# Optimizing a Trainium2 kernel written in Bass

```python
import jax, jax.numpy as jnp
from jax import lax
import numpy as np

D_MODEL = 1024
BATCH = 1
SEQ = 256
DEPTH = 2
DEC_BATCH = 8
DEC_SEQ = 1
PAST_LEN = 2048
PAGE_SIZE = 128

N_MIXERS = 2
N_POOL_LAYERS = (DEPTH + 1) // 2
N_CONV_LAYERS = DEPTH // 2
N_META = 16
POOL_WINDOWS = (2, 4, 8, 16)
N_POOL_GROUPS = len(POOL_WINDOWS)
POOL_GROUP_DIM = D_MODEL // N_POOL_GROUPS
POOL_STATE = max(POOL_WINDOWS) - 1
CONV_WIDTH = 31
CONV_STATE = CONV_WIDTH - 1
N_GROUPS = 4
EXPERTS_PER_GROUP = 8
N_EXPERTS = N_GROUPS * EXPERTS_PER_GROUP
TOP_K = 2
D_EXPERT = D_MODEL // 2
MOE_BLOCK = 128
ALPHA = (2.0 * DEPTH) ** 0.25
BETA = (8.0 * DEPTH) ** -0.25
LN_EPS = 1e-5

kernel_name = 'hybrid_pool_conformer_hmoe_decoder_step'

def layer_norm(x, g, b):
    xf = x.astype(jnp.float32)
    mu = jnp.mean(xf, axis=-1, keepdims=True)
    var = jnp.mean(jnp.square(xf - mu), axis=-1, keepdims=True)
    y = (xf - mu) * lax.rsqrt(var + LN_EPS) * g.astype(jnp.float32) + b.astype(jnp.float32)
    return y.astype(x.dtype)

def pool_mixer(x, prefix, pos0, w_pool, scale):
    B, L, D = x.shape
    xcat = jnp.concatenate([prefix.astype(x.dtype), x], axis=1)
    c = jnp.cumsum(xcat.astype(jnp.float32), axis=1)
    c = jnp.pad(c, ((0, 0), (1, 0), (0, 0)))
    pos = pos0 + jnp.arange(L)
    end = POOL_STATE + 1
    means = []
    for g, w in enumerate(POOL_WINDOWS):
        lo, hi = g * POOL_GROUP_DIM, (g + 1) * POOL_GROUP_DIM
        s = c[:, end:end + L, lo:hi] - c[:, end - w:end - w + L, lo:hi]
        cnt = jnp.minimum(pos + 1, w).astype(jnp.float32)
        means.append(s / cnt[None, :, None])
    mean = jnp.stack(means, axis=2)
    xg = x.reshape(B, L, N_POOL_GROUPS, POOL_GROUP_DIM).astype(jnp.float32)
    diff = (mean - xg).astype(x.dtype)
    y = jnp.einsum('blgc,gcd->blgd', diff, w_pool).reshape(B, L, D)
    return y * scale, xcat[:, -POOL_STATE:]

def conv_mixer(x, prefix, w_glu, b_glu, w_dw, b_dw, ln_g, ln_b, w_pw, b_pw):
    h = jnp.einsum('bld,de->ble', x, w_glu) + b_glu
    a, gate = jnp.split(h, 2, axis=-1)
    u = a * jax.nn.sigmoid(gate)
    ucat = jnp.concatenate([prefix.astype(u.dtype), u], axis=1)
    v = lax.conv_general_dilated(ucat, w_dw[:, None, :].astype(u.dtype), window_strides=(1,),
                                 padding='VALID', dimension_numbers=('NWC', 'WIO', 'NWC'),
                                 feature_group_count=D_MODEL) + b_dw
    v = jax.nn.silu(layer_norm(v, ln_g, ln_b))
    y = jnp.einsum('bld,de->ble', v, w_pw) + b_pw
    return y, ucat[:, -CONV_STATE:]

def hier_moe(x, w_rg, w_re, w_gate, w_up, w_down):
    T, D = x.shape
    pg = jax.nn.softmax(jnp.einsum('td,dg->tg', x, w_rg).astype(jnp.float32), axis=-1)
    p_grp, g_top = lax.top_k(pg, 1)
    le = jnp.einsum('td,de->te', x, w_re).astype(jnp.float32).reshape(T, N_GROUPS, EXPERTS_PER_GROUP)
    le_g = le[jnp.arange(T), g_top[:, 0]]
    pe = jax.nn.softmax(le_g, axis=-1)
    pe_top, e_top = lax.top_k(pe, TOP_K)
    gates = p_grp * (pe_top / jnp.sum(pe_top, axis=-1, keepdims=True))
    experts = (g_top * EXPERTS_PER_GROUP + e_top).astype(jnp.int32)

    A = T * TOP_K
    flat_e = experts.reshape(-1)
    order = jnp.argsort(flat_e)
    sorted_e = flat_e[order]
    counts = jnp.bincount(flat_e, length=N_EXPERTS)
    padded = ((counts + MOE_BLOCK - 1) // MOE_BLOCK) * MOE_BLOCK
    padded_ends = jnp.cumsum(padded)
    padded_starts = padded_ends - padded
    starts = jnp.cumsum(counts) - counts
    dest = padded_starts[sorted_e] + (jnp.arange(A) - starts[sorted_e])
    n_blocks = -(-A // MOE_BLOCK) + N_EXPERTS
    n_slots = n_blocks * MOE_BLOCK
    token_of_slot = jnp.full((n_slots,), T, jnp.int32).at[dest].set((order // TOP_K).astype(jnp.int32))
    block_expert = jnp.minimum(jnp.searchsorted(padded_ends, jnp.arange(n_blocks) * MOE_BLOCK, side='right'),
                               N_EXPERTS - 1).astype(jnp.int32)
    x_pad = jnp.concatenate([x, jnp.zeros((1, D), x.dtype)], axis=0)
    xs = x_pad[token_of_slot].reshape(n_blocks, MOE_BLOCK, D)

    def expert_block(args):
        xb, e = args
        hb = jax.nn.silu(xb @ w_gate[e]) * (xb @ w_up[e])
        return hb @ w_down[e]

    ys = lax.map(expert_block, (xs, block_expert)).reshape(n_slots, D)
    slot_of_assign = jnp.zeros((A,), jnp.int32).at[order].set(dest.astype(jnp.int32))
    y_assign = ys[slot_of_assign].reshape(T, TOP_K, D)
    return jnp.einsum('tkd,tk->td', y_assign, gates.astype(y_assign.dtype))

def run_trunk(h, pool_state, conv_state, pos0, w_pool, pool_scale, w_glu, b_glu, w_dw, b_dw,
              conv_ln_g, conv_ln_b, w_pw, b_pw, ln_mix_g, ln_mix_b, ln_ffn_g, ln_ffn_b,
              w_router_group, w_router_expert, w_gate, w_up, w_down):
    new_pool, new_conv = [], []
    for i in range(DEPTH):
        j = i // N_MIXERS
        if i % N_MIXERS == 0:
            m, st = pool_mixer(h, pool_state[j], pos0, w_pool[j], pool_scale[j])
            new_pool.append(st)
        else:
            m, st = conv_mixer(h, conv_state[j], w_glu[j], b_glu[j], w_dw[j], b_dw[j],
                               conv_ln_g[j], conv_ln_b[j], w_pw[j], b_pw[j])
            new_conv.append(st)
        h = layer_norm(ALPHA * h + m, ln_mix_g[i], ln_mix_b[i])
        B, L, D = h.shape
        f = hier_moe(h.reshape(B * L, D), w_router_group[i], w_router_expert[i],
                     w_gate[i], w_up[i], w_down[i]).reshape(B, L, D)
        h = layer_norm(ALPHA * h + f, ln_ffn_g[i], ln_ffn_b[i])
    return h, jnp.stack(new_pool, axis=0), jnp.stack(new_conv, axis=0)

def setup_inputs(seed: int = 0) -> dict:
    key = jax.random.key(seed)
    ks = jax.random.split(key, 26)
    n = lambda k, s: jax.random.normal(k, s, jnp.float32)
    D, F = D_MODEL, D_EXPERT
    return {
        'x_prompt': n(ks[0], (BATCH, SEQ, D)),
        'x_sample': n(ks[1], (DEC_BATCH, DEC_SEQ, D)),
        'state_pool': n(ks[2], (N_POOL_LAYERS, DEC_BATCH, POOL_STATE, D)),
        'state_conv': 0.5 * n(ks[3], (N_CONV_LAYERS, DEC_BATCH, CONV_STATE, D)),
        'meta': n(ks[4], (N_META, D)),
        'w_pool': n(ks[5], (N_POOL_LAYERS, N_POOL_GROUPS, POOL_GROUP_DIM, POOL_GROUP_DIM)) * (POOL_GROUP_DIM ** -0.5) * BETA,
        'pool_scale': 1.0 + 0.1 * n(ks[6], (N_POOL_LAYERS, D)),
        'w_glu': n(ks[7], (N_CONV_LAYERS, D, 2 * D)) * D ** -0.5,
        'b_glu': 0.02 * n(ks[8], (N_CONV_LAYERS, 2 * D)),
        'w_dw': n(ks[9], (N_CONV_LAYERS, CONV_WIDTH, D)) * CONV_WIDTH ** -0.5,
        'b_dw': 0.02 * n(ks[10], (N_CONV_LAYERS, D)),
        'conv_ln_g': 1.0 + 0.1 * n(ks[11], (N_CONV_LAYERS, D)),
        'conv_ln_b': 0.02 * n(ks[12], (N_CONV_LAYERS, D)),
        'w_pw': n(ks[13], (N_CONV_LAYERS, D, D)) * (D ** -0.5) * BETA,
        'b_pw': 0.02 * n(ks[14], (N_CONV_LAYERS, D)),
        'ln_mix_g': 1.0 + 0.1 * n(ks[15], (DEPTH, D)),
        'ln_mix_b': 0.02 * n(ks[16], (DEPTH, D)),
        'ln_ffn_g': 1.0 + 0.1 * n(ks[17], (DEPTH, D)),
        'ln_ffn_b': 0.02 * n(ks[18], (DEPTH, D)),
        'w_router_group': n(ks[19], (DEPTH, D, N_GROUPS)) * D ** -0.5,
        'w_router_expert': n(ks[20], (DEPTH, D, N_EXPERTS)) * D ** -0.5,
        'w_gate': n(ks[21], (DEPTH, N_EXPERTS, D, F)) * D ** -0.5,
        'w_up': n(ks[22], (DEPTH, N_EXPERTS, D, F)) * D ** -0.5,
        'w_down': n(ks[23], (DEPTH, N_EXPERTS, F, D)) * (F ** -0.5) * BETA,
    }

def reference(x_prompt, x_sample, state_pool, state_conv, meta, w_pool, pool_scale, w_glu, b_glu,
              w_dw, b_dw, conv_ln_g, conv_ln_b, w_pw, b_pw, ln_mix_g, ln_mix_b, ln_ffn_g, ln_ffn_b,
              w_router_group, w_router_expert, w_gate, w_up, w_down):
    B = x_prompt.shape[0]
    meta_b = jnp.broadcast_to(meta.astype(x_prompt.dtype)[None], (B, N_META, D_MODEL))
    h_p = jnp.concatenate([meta_b, x_prompt], axis=1)
    zero_pool = jnp.zeros((N_POOL_LAYERS, B, POOL_STATE, D_MODEL), x_prompt.dtype)
    zero_conv = jnp.zeros((N_CONV_LAYERS, B, CONV_STATE, D_MODEL), x_prompt.dtype)
    h_p, pool_p, conv_p = run_trunk(h_p, zero_pool, zero_conv, 0, w_pool, pool_scale, w_glu, b_glu,
                                    w_dw, b_dw, conv_ln_g, conv_ln_b, w_pw, b_pw, ln_mix_g, ln_mix_b,
                                    ln_ffn_g, ln_ffn_b, w_router_group, w_router_expert,
                                    w_gate, w_up, w_down)
    y_prompt = h_p[:, N_META:]
    h_s, pool_s, conv_s = run_trunk(x_sample, state_pool, state_conv, PAST_LEN, w_pool, pool_scale,
                                    w_glu, b_glu, w_dw, b_dw, conv_ln_g, conv_ln_b, w_pw, b_pw,
                                    ln_mix_g, ln_mix_b, ln_ffn_g, ln_ffn_b, w_router_group,
                                    w_router_expert, w_gate, w_up, w_down)
    return (y_prompt, h_s, pool_p, pool_s, conv_p, conv_s)


_drawn_inputs = setup_inputs


def setup_inputs(seed=0):
    import zlib

    import numpy as np

    out = dict(_drawn_inputs(seed))
    spreads = {}
    factors = {'b_glu': 2.709, 'b_dw': 5.045, 'conv_ln_b': 8.0, 'b_pw': 3.501}
    for name, (base, spread) in spreads.items():
        noise = np.random.default_rng([zlib.crc32(name.encode()), seed]).standard_normal(out[name].shape)
        drawn = base * np.exp(spread * noise) if base else spread * noise
        out[name] = __import__('jax').numpy.asarray(drawn.astype(out[name].dtype))
    for name, factor in factors.items():
        out[name] = (out[name] * factor).astype(out[name].dtype)
    return out
```

```python
import concourse.bass as bass
from concourse import mybir
from concourse.alu_op_type import AluOpType as ALU
from contextlib import ExitStack
import numpy as np

D = 1024
F = D // 2
P = 128
KD, KF = D // P, F // P
HALF = 512
META, SEQ, NSAMP = 16, 256, 8
NPROMPT = META + SEQ
T = NPROMPT + NSAMP
TILES = [(0, 128), (128, 128), (256, 24)]
WINDOWS = (2, 4, 8, 16)
NPG, PGD = len(WINDOWS), D // len(WINDOWS)
PSTATE, CSTATE, TAPS = 15, 30, 31
NG, EPG = 4, 8
NE = NG * EPG
QUAD = 4
CAP = P // QUAD
NQ = NE // QUAD
DEPTH = 2
ALPHA = (2.0 * DEPTH) ** 0.25
EPS = 1e-5
CHUNK = 4096
RING = 8
QCHUNKS = 12
LOOPS = NQ // 2
MIX_CHUNKS = 6
BASE = [0, NQ * QCHUNKS + MIX_CHUNKS]
MIX_BASE = NQ * QCHUNKS
BIG = 64.0

C_ID, C_UP, C_ONE, C_IOTA, C_SELB, C_MEAN = 0, 128, 256, 384, 416, 420
C_END = 548
B_0, B_1, B_2, B_S, B_END = 0, 4 * 144, 8 * 144, 8 * 144 + 4 * 24, 8 * 144 + 4 * 24 + 4 * 8
R_BDW, R_G, R_B, R_BA, R_BG, R_N = 31, 32, 33, 34, 35, 36


def constants():
    c = np.zeros((P, C_END), np.float32)
    c[:, C_ID:C_ID + P] = np.eye(P)
    c[:, C_UP:C_UP + P] = np.triu(np.ones((P, P)), 1)
    c[:, C_ONE:C_ONE + P] = 1
    c[:, C_IOTA:C_IOTA + CAP] = np.arange(1, CAP + 1)
    for b in range(4):
        c[b * CSTATE:(b + 1) * CSTATE, C_SELB + b] = 1
    c[:, C_MEAN:C_MEAN + P] = 1.0 / D
    bands = np.zeros((P, B_END), np.float32)
    for g, w in enumerate(WINDOWS):
        for p in range(P):
            for j in range(144):
                for at, off in ((B_0, 0), (B_1, P)):
                    if 0 <= j - p < w:
                        bands[p, at + g * 144 + j] = 1.0 / min(off + j + 1, w)
                    if j == p:
                        bands[p, at + g * 144 + j] -= 1
        for p in range(META):
            for j in range(p, min(p + w, META)):
                bands[p, B_2 + g * 24 + j] = 1.0 / w
            bands[p, B_2 + g * 24 + p] -= 1
        for b in range(NSAMP):
            bands[META + b, B_2 + g * 24 + META + b] = 1.0 / w - 1
            for r in range(PSTATE + 1 - w, PSTATE):
                bands[b * PSTATE + r, B_S + g * 8 + b] = 1.0 / w
    return c, bands


def build(nc, a, outs):
    fp32, i32 = mybir.dt.float32, mybir.dt.int32
    ACT = mybir.ActivationFunctionType
    AX = mybir.AxisListType
    y_prompt, y_sample, pool_p, pool_s, conv_p, conv_s = outs

    ctx = ExitStack()
    with ctx:
        def sb(name, shape, dt=fp32):
            return ctx.enter_context(nc.sbuf_tensor(name, shape, dt))

        def sem(name):
            return ctx.enter_context(nc.semaphore(name))

        ring = sb("ring", [P, RING, CHUNK])
        cst = sb("cst", [P, C_END])
        x = sb("x", [P, 3, D])
        z = sb("z", [P, 3, D])
        xT = sb("xT", [P, KD, T])
        gb = sb("gb", [P, 2, D])
        wr = sb("wr", [P, DEPTH, KD, 36])
        lg = sb("lg", [P, 3, 36])
        st = sb("st", [P, 3, 12])
        mv = sb("mv", [P, 3, 2])
        rs = sb("rs", [P, 3, 2])
        sm = sb("sm", [P, 16, 3, 8])
        assign = sb("assign", [P, 3, NE])
        gates = sb("gates", [P, 3, NE])
        slot1 = sb("slot1", [P, 3, NE])
        over = sb("over", [P, 3, NE])
        le4 = sb("le4", [P, 3, EPG, NG])
        cnt = sb("cnt", [1, NE])
        cntf = sb("cntf", [1, 1])
        most = sb("most", [1, 1], i32)
        chan = sb("chan", [P, KD, R_N])
        vstate = sb("vstate", [P, KD, NSAMP])
        bpw = sb("bpw", [1, D])
        U = sb("U", [P, 5760])

        def view(at, n, **k):
            v = U[:, at:at + n]
            return v.rearrange(k.pop("r"), **k) if k else v

        wp = view(0, 2048, r="p (g k n) -> p g k n", g=NPG, k=2)
        cs_raw = view(2048, 2 * D, r="p (h n) -> p h n", h=2)
        wrep = view(2048 + 2 * D, D)
        zflat = z[:, :, :].rearrange("p i n -> p (i n)")
        bands = zflat[:, 0:B_END]
        pstate = zflat[:, B_END:B_END + D]
        crow = xT[0:R_N, :, :].rearrange("p a b -> p (a b)")[:, 0:D]
        pscale = gb[:, 0, :]
        onehot = view(0, 384, r="p (i s) -> p i s", i=3)
        gated = view(384, 384, r="p (i s) -> p i s", i=3)
        gT = view(768, T)
        xg = view(1056, 1024, r="p (k s) -> p k s", k=KD)
        sil = view(2080, F)
        h = view(2592, F)
        hT = view(3104, F, r="p (k s) -> p k s", k=KF)
        ye = view(3616, D)
        UW = CSTATE + T
        u = view(0, KD * UW, r="p (k n) -> p k n", k=KD)
        v = zflat[:, 0:KD * T].rearrange("p (k n) -> p k n", k=KD)
        sq = view(KD * UW, KD * T, r="p (k n) -> p k n", k=KD)
        sg = sq
        urow = view(KD * (UW + T), D)
        rstd = sb("rstd", [P, T])

        ps = ctx.enter_context(nc.psum_tensor("ps", [P, 8, HALF], fp32))

        ident = cst[:, C_ID:C_ID + P]
        upper = cst[:, C_UP:C_UP + P]
        ones = cst[:, C_ONE:C_ONE + P]
        iota1 = cst[:, C_IOTA:C_IOTA + CAP]
        mean_w = cst[:, C_MEAN:C_MEAN + P]

        filled = [sem(f"filled{s}") for s in range(RING)]
        ring_free = sem("ring_free")
        x_in, w_in, prep_in, gb_in = (sem(n) for n in ("x_in", "w_in", "prep_in", "gb_in"))
        outs_done = sem("outs_done")
        zeroed = sem("zeroed")
        wp_scaled = sem("wp_scaled")
        state_mul = sem("state_mul")
        diff_done, diff_a, diff_d, pooled = (sem(n) for n in ("diff_done", "diff_a", "diff_d", "pooled"))
        chan_turned, chan_ready, vstate_done = (sem(n) for n in ("chan_turned", "chan_ready", "vstate_done"))
        prep_done = sem("prep_done")
        chain = sem("chain")
        root_in, root_out, stats_ready, centred, normed, crt_in, crt_out = (
            sem(n) for n in ("root_in", "root_out", "stats_ready", "centred", "normed", "crt_in", "crt_out"))
        turned, xT_a, xT_d = (sem(n) for n in ("turned", "xT_a", "xT_d"))
        logits_done, exp_in, exp_out, routed, placed, slots_ready, most_ready = (
            sem(n) for n in ("logits_done", "exp_in", "exp_out", "routed", "placed", "slots_ready", "most_ready"))
        residual = sem("residual")
        onehot_ready, gated_ready, dispatched, gT_turned, gT_ready, xg_a, xg_d = (
            sem(n) for n in ("onehot_ready", "gated_ready", "dispatched", "gT_turned", "gT_ready", "xg_a", "xg_d"))
        silu_done, h_ready, hT_turned, hT_ready, ye_a, ye_d, combined, added = (
            sem(n) for n in ("silu_done", "h_ready", "hT_turned", "hT_ready", "ye_a", "ye_d", "combined", "added"))
        glu_done, sig_ready, u_ready, conv_step, conv_done = (
            sem(n) for n in ("glu_done", "sig_ready", "u_ready", "conv_step", "conv_done"))
        mean_done, cent_ready, sq_ready, var_done, vn_ready, act_ready, pw_done, urow_turned, urow_ready = (
            sem(n) for n in ("mean_done", "cent_ready", "sq_ready", "var_done", "vn_ready", "act_ready",
                             "pw_done", "urow_turned", "urow_ready"))
        fb = []
        for L in range(DEPTH):
            fb.append({n: sem(f"over{L}_{n}") for n in (
                "fill0", "fill1", "fill2", "used", "hidden", "silu", "h", "turned", "hT", "down", "added")})

        block = ctx.enter_context(nc.Block())

        def ring_slot(n):
            return n % RING

        def fills(n):
            return 32 * (n // RING + 1)

        def used_up(n):
            return RING + n + 1

        @block.sync
        def _(sp):
            mt, xp, xs = a["meta"], a["x_prompt"], a["x_sample"]
            sp.dma_start(x[0:META, 0, :], mt).then_inc(x_in, 16)
            sp.dma_start(x[META:P, 0, :], xp[0, 0:112, :]).then_inc(x_in, 16)
            sp.dma_start(x[:, 1, :], xp[0, 112:240, :]).then_inc(x_in, 16)
            sp.dma_start(x[0:16, 2, :], xp[0, 240:256, :]).then_inc(x_in, 16)
            sp.dma_start(x[16:24, 2, :], xs[:, 0, :]).then_inc(x_in, 16)
            sp.dma_start(pstate[0:120, :], a["state_pool"][0].rearrange("b j d -> (b j) d")).then_inc(x_in, 16)
            sp.dma_start(bands, a["bands"]).then_inc(x_in, 16)
            sp.dma_start(wp, a["w_pool"][0].rearrange("g (k p) n -> p g k n", p=P)).then_inc(w_in, 16)
            sp.dma_start(pscale, a["pool_scale"][0:1, :].broadcast_to([P, D])).then_inc(w_in, 16)
            sp.dma_start(cst[:, :], a["cst"]).then_inc(w_in, 16)
            sp.dma_start(crow[0:TAPS, :], a["w_dw"][0]).then_inc(prep_in, 16)
            sp.dma_start(crow[R_BDW:R_BDW + 1, :], a["b_dw"]).then_inc(prep_in, 16)
            sp.dma_start(crow[R_G:R_G + 1, :], a["conv_ln_g"]).then_inc(prep_in, 16)
            sp.dma_start(crow[R_B:R_B + 1, :], a["conv_ln_b"]).then_inc(prep_in, 16)
            sp.dma_start(crow[R_BA:R_BG + 1, :], a["b_glu"].rearrange("o (h n) -> (o h) n", h=2)).then_inc(prep_in, 16)
            sp.dma_start(cs_raw[0:120, :, :], a["state_conv"][0].rearrange("(h b) j d -> (b j) h d", h=2)).then_inc(prep_in, 16)
            for b in range(4):
                sp.dma_start(wrep[b * CSTATE:(b + 1) * CSTATE, :], a["w_dw"][0, 0:CSTATE, :]).then_inc(prep_in, 16)
            sp.sem_inc(ring_free, RING)

            def load(n, parts, count=None):
                sp.wait_ge(ring_free, n + 1 if count is None else count)
                for dst, src in parts:
                    sp.dma_start(dst, src).then_inc(filled[ring_slot(n)], 32 // len(parts))

            def experts(L):
                up = [a[w][L].rearrange("e (k p) f -> p e k f", p=P) for w in ("w_gate", "w_up")]
                down = a["w_down"][L].rearrange("e (k p) n -> p e k n", p=P)
                with sp.Fori(0, LOOPS) as it:
                    for b in range(2):
                        first = sp.snap(it * 8 + 4 * b)
                        for c in range(QCHUNKS):
                            n = BASE[L] + QCHUNKS * b + c
                            if c < 8:
                                dst = ring[:, ring_slot(n), :].rearrange("p (e k f) -> p e k f", e=QUAD, k=2)
                                parts = [(dst[:, :, k, :], up[c // 4][:, bass.ds(first, QUAD), 2 * (c % 4) + k, :])
                                         for k in range(2)]
                            else:
                                dst = ring[:, ring_slot(n), :].rearrange("p (e f) -> p e f", e=QUAD)
                                parts = [(dst, down[:, bass.ds(first, QUAD), c - 8, :])]
                            load(n, parts, it * (2 * QCHUNKS) + (n + 1))

            def overflow(L):
                s = fb[L]
                sp.wait_ge(most_ready, L + 1)
                count = sp.value_load(most[0:1, 0:1], min_val=0, max_val=T)
                with sp.If(count > CAP):
                    sp.wait_ge(ring_free, RING + BASE[L] + NQ * QCHUNKS)
                    with sp.Fori(0, NE) as e:
                        ee = sp.snap(e)
                        for m, w in enumerate(("w_gate", "w_up", "w_down")):
                            kk = 4 if m == 2 else 8
                            src = a[w][L][bass.ds(ee, 1), :, :].rearrange("o (k p) f -> p (o k) f", p=P)
                            dst = ring[:, m, :].rearrange("p (k f) -> p k f", k=kk)
                            sp.wait_ge(s["used"], e + 1)
                            sp.dma_start(dst, src).then_inc(s[f"fill{m}"], 16)
                    sp.wait_ge(s["used"], NE + 1)

            experts(0)
            overflow(0)
            glu = a["w_glu"][0].rearrange("(k p) (h n) -> p k h n", p=P, h=2)
            for j in range(4):
                n = MIX_BASE + j
                dst = ring[:, ring_slot(n), :].rearrange("p (k h n) -> p k h n", k=KD, h=2)
                load(n, [(dst[:, :, hh, :], glu[:, :, hh, 256 * j:256 * j + 256]) for hh in range(2)])
            for j in range(2):
                n = MIX_BASE + 4 + j
                load(n, [(ring[:, ring_slot(n), :].rearrange("p (k n) -> p k n", k=4),
                          a["w_pw"][0, 512 * j:512 * j + 512, :].rearrange("(k p) n -> p k n", p=P))])
            experts(1)
            overflow(1)
            sp.wait_ge(normed, 10)
            sp.dma_start(y_prompt[0, 0:112, :], x[META:P, 0, :]).then_inc(outs_done, 16)
            sp.wait_ge(normed, 11)
            sp.dma_start(y_prompt[0, 112:240, :], x[:, 1, :]).then_inc(outs_done, 16)
            sp.wait_ge(normed, 12)
            sp.dma_start(y_prompt[0, 240:256, :], x[0:16, 2, :]).then_inc(outs_done, 16)
            sp.dma_start(y_sample[:, 0, :], x[16:24, 2, :]).then_inc(outs_done, 16)
            sp.wait_ge(outs_done, 16 * 10)

        @block.gpsimd
        def _(pool):
            for t in (lg, assign, gates, slot1, over, sm):
                pool.memset(t[:], 0.0).then_inc(zeroed, 1)
            pool.memset(rstd[:], 0.0).then_inc(zeroed, 1)
            pool.wait_ge(prep_in, 16 * 15)
            for hh in range(2):
                pool.tensor_tensor(out=cs_raw[0:120, hh, :], in0=cs_raw[0:120, hh, :], in1=wrep[0:120, :],
                                   op=ALU.mult).then_inc(state_mul, 1)

        @block.scalar
        def _(act):
            for L in range(DEPTH):
                act.dma_start(wr[:, L, :, 0:NG], a["w_router_group"][L].rearrange("(k p) n -> p k n", p=P)).then_inc(prep_in, 16)
                act.dma_start(wr[:, L, :, NG:NG + NE], a["w_router_expert"][L].rearrange("(k p) n -> p k n", p=P)).then_inc(prep_in, 16)
            act.dma_start(bpw[:, :], a["b_pw"]).then_inc(prep_in, 16)
            act.dma_start(pool_p[0, 0], a["x_prompt"][0, SEQ - PSTATE:SEQ, :]).then_inc(outs_done, 16)
            act.dma_start(pool_s[0, :, 0:PSTATE - 1, :], a["state_pool"][0, :, 1:PSTATE, :]).then_inc(outs_done, 16)
            act.dma_start(pool_s[0, :, PSTATE - 1, :], a["x_sample"][:, 0, :]).then_inc(outs_done, 16)
            act.dma_start(conv_s[0, :, 0:CSTATE - 1, :], a["state_conv"][0, :, 1:CSTATE, :]).then_inc(outs_done, 16)

            def load_gb(n):
                g, b = (("ln_mix_g", "ln_mix_b"), ("ln_ffn_g", "ln_ffn_b"))[n % 2]
                L = n // 2
                if n == 0:
                    act.wait_ge(wp_scaled, 1)
                else:
                    act.wait_ge(normed, 3 * n)
                act.dma_start(gb[:, 0, :], a[g][L:L + 1, :].broadcast_to([P, D])).then_inc(gb_in, 16)
                act.dma_start(gb[:, 1, :], a[b][L:L + 1, :].broadcast_to([P, D])).then_inc(gb_in, 16)

            def centre(n):
                for i, (t0, tn) in enumerate(TILES):
                    act.wait_ge(root_in, 3 * n + i + 1)
                    act.activation(mv[0:tn, i, 1:2], mv[0:tn, i, 1:2], ACT.Sqrt).then_inc(root_out, 1)
                for i, (t0, tn) in enumerate(TILES):
                    act.wait_ge(stats_ready, 3 * n + i + 1)
                    act.activation(z[0:tn, i, :], z[0:tn, i, :], ACT.Identity,
                                   bias=rs[0:tn, i, 1:2], scale=rs[0:tn, i, 0:1]).then_inc(centred, 1)

            def turn(m):
                for n, (i, k) in enumerate(((0, 0), (1, 0), (2, 0))):
                    act.wait_ge(turned, 5 * m + 2 * n + 1)
                    t0, tn = TILES[i]
                    if i < 2:
                        act.activation(xT[:, 0:4, t0:t0 + tn], ps[:, 2 * i, :].rearrange("p (k t) -> p k t", k=4), ACT.Copy).then_inc(xT_a, 1)
                    else:
                        act.activation(xT[:, :, t0:t0 + tn], ps[:, 4, 0:KD * tn].rearrange("p (k t) -> p k t", k=KD), ACT.Copy).then_inc(xT_a, 1)

            def route(L):
                turn(2 * L)
                for n in range(2):
                    act.wait_ge(exp_in, 2 * L + n + 1)
                    t = sm[:, 0, :, 0:NG] if n == 0 else sm[:, 9, :, 0:1]
                    o = sm[:, 1, :, 0:NG] if n == 0 else sm[:, 10, :, 0:1]
                    act.activation(o, t, ACT.Exp).then_inc(exp_out, 1)
                act.wait_ge(normed, 6 * L + 3)
                for i, (t0, tn) in enumerate(TILES):
                    act.activation(z[0:tn, i, :], x[0:tn, i, :], ACT.Copy, scale=ALPHA).then_inc(residual, 1)

            def experts(L):
                with act.Fori(0, LOOPS) as it:
                    for b in range(2):
                        q = NQ * L + b + 1
                        done = it * 2 + q
                        act.wait_ge(dispatched, it * 4 + (2 * q - 1))
                        act.activation(xg[:, 0:4, :], ps[:, 6, :].rearrange("p (k s) -> p k s", k=4), ACT.Copy).then_inc(xg_a, 1)
                        through = it * (2 * QCHUNKS) + used_up(BASE[L] + QCHUNKS * b - 1)
                        act.wait_ge(ring_free, through + 4)
                        act.activation(sil, ps[:, 0, :], ACT.Silu).then_inc(silu_done, 1)
                        act.wait_ge(hT_turned, done)
                        act.activation(hT, ps[:, 5, :].rearrange("p (k s) -> p k s", k=KF), ACT.Copy).then_inc(hT_ready, 1)
                        act.wait_ge(ring_free, through + 12)
                        act.activation(ye[:, 0:HALF], ps[:, 2, :], ACT.Copy).then_inc(ye_a, 1)

            def overflow(L):
                s = fb[L]
                act.wait_ge(most_ready, L + 1)
                count = act.value_load(most[0:1, 0:1], min_val=0, max_val=T)
                with act.If(count > CAP):
                    with act.Fori(0, NE) as e:
                        for i, (t0, tn) in enumerate(TILES):
                            act.wait_ge(s["hidden"], e * 3 + (i + 1))
                            act.activation(sil[0:tn, :], ps[0:tn, 0, :], ACT.Silu).then_inc(s["silu"], 1)
                            act.wait_ge(s["turned"], e * 3 + (i + 1))
                            act.activation(hT, ps[:, 5, :].rearrange("p (k s) -> p k s", k=KF), ACT.Copy).then_inc(s["hT"], 1)

            for c in range(0, KD, 2):
                act.wait_ge(diff_done, c + 1)
                if c == 0:
                    act.wait_ge(chan_turned, 1)
                act.activation(xT[:, c, :], ps[:, c, 0:T], ACT.Copy).then_inc(diff_a, 1)
            load_gb(0)
            centre(0)
            load_gb(1)
            route(0)
            experts(0)
            overflow(0)
            centre(1)
            load_gb(2)
            turn(1)
            for e in range(KD):
                if e % 2:
                    act.wait_ge(ring_free, used_up(MIX_BASE + e // 2))
                else:
                    act.wait_ge(glu_done, e // 2 + 1)
                act.activation(sg[:, e, :], ps[:, 2 * (e % 4) + 1, 0:T], ACT.Sigmoid,
                               bias=chan[:, e, R_BG:R_BG + 1]).then_inc(sig_ready, 1)
            for e in range(KD):
                act.wait_ge(cent_ready, e // 4 + 1)
                act.activation(sq[:, e, :], v[:, e, :], ACT.Square).then_inc(sq_ready, 1)
            act.wait_ge(crt_in, 1)
            act.activation(rstd[:, :], rstd[:, :], ACT.Sqrt).then_inc(crt_out, 1)
            for e in range(KD):
                act.wait_ge(vn_ready, e // 4 + 1)
                act.activation(sq[:, e, :], v[:, e, :], ACT.Silu, bias=chan[:, e, R_B:R_B + 1],
                               scale=chan[:, e, R_G:R_G + 1]).then_inc(act_ready, 1)
            act.wait_ge(urow_ready, 2)
            act.dma_start(conv_p[0, 0], urow[0:CSTATE, :]).then_inc(outs_done, 16)
            act.dma_start(conv_s[0, :, CSTATE - 1, :], urow[CSTATE:CSTATE + NSAMP, :]).then_inc(outs_done, 16)
            centre(2)
            load_gb(3)
            act.wait_ge(outs_done, 16 * 6)
            route(1)
            experts(1)
            overflow(1)
            centre(3)

        @block.vector
        def _(dve):
            steps = [0]

            def link(ins):
                steps[0] += 1
                ins.then_inc(chain, 1)
                dve.wait_ge(chain, steps[0])

            def layer_norm(n):
                for i, (t0, tn) in enumerate(TILES):
                    if n == 2:
                        residual_pw(i)
                    if n == 0:
                        residual_pool(i)
                    for k in range(2):
                        link(dve.bn_stats(st[0:tn, i, 6 * k:6 * k + 6], z[0:tn, i, HALF * k:HALF * k + HALF]))
                    link(dve.bn_aggr(mv[0:tn, i, :], st[0:tn, i, :]))
                    dve.tensor_scalar(mv[0:tn, i, 1:2], mv[0:tn, i, 1:2], EPS, None, ALU.add).then_inc(root_in, 1)
                for i, (t0, tn) in enumerate(TILES):
                    dve.wait_ge(root_out, 3 * n + i + 1)
                    link(dve.reciprocal(rs[0:tn, i, 0:1], mv[0:tn, i, 1:2]))
                    dve.tensor_scalar(rs[0:tn, i, 1:2], mv[0:tn, i, 0:1], rs[0:tn, i, 0:1], -1.0,
                                      ALU.mult, ALU.mult).then_inc(stats_ready, 1)
                dve.wait_ge(gb_in, 32 * (n + 1))
                for i, (t0, tn) in enumerate(TILES):
                    dve.wait_ge(centred, 3 * n + i + 1)
                    link(dve.tensor_tensor(out=z[0:tn, i, :], in0=z[0:tn, i, :], in1=gb[0:tn, 0, :], op=ALU.mult))
                    dve.tensor_tensor(out=x[0:tn, i, :], in0=z[0:tn, i, :], in1=gb[0:tn, 1, :], op=ALU.add).then_inc(normed, 1)

            def residual_pool(i):
                t0, tn = TILES[i]
                dve.wait_ge(pooled, i + 1)
                link(dve.scalar_tensor_tensor(out=z[0:tn, i, :].rearrange("p (h n) -> p h n", h=2),
                                              in0=x[0:tn, i, :].rearrange("p (h n) -> p h n", h=2), scalar=ALPHA,
                                              in1=ps[0:tn, 2 * i:2 * i + 2, :], op0=ALU.mult, op1=ALU.add))

            def residual_pw(i):
                t0, tn = TILES[i]
                if i < 2:
                    dve.wait_ge(pw_done, i + 1)
                else:
                    dve.wait_ge(ring_free, used_up(MIX_BASE + MIX_CHUNKS - 1))
                link(dve.scalar_tensor_tensor(out=z[0:tn, i, :].rearrange("p (h n) -> p h n", h=2),
                                              in0=x[0:tn, i, :].rearrange("p (h n) -> p h n", h=2), scalar=ALPHA,
                                              in1=ps[0:tn, 2 * i:2 * i + 2, :], op0=ALU.mult, op1=ALU.add))

            def turn(m):
                for i in range(2):
                    t0, tn = TILES[i]
                    dve.wait_ge(turned, 5 * m + 2 * i + 2)
                    dve.tensor_copy(xT[:, 4:8, t0:t0 + tn], ps[:, 2 * i + 1, :].rearrange("p (k t) -> p k t", k=4)).then_inc(xT_d, 1)

            def first_best(val, is_zero, out):
                n = val.shape[2]
                cand, low = sm[:, 12, :, 0:n], sm[:, 13, :, 0:1]
                idx = iota1[:, 0:n].unsqueeze(1).broadcast_to([P, 3, n])
                link(dve.tensor_scalar(cand, val, 0.0, -BIG, ALU.is_equal, ALU.mult))
                link(dve.tensor_tensor(out=cand, in0=cand, in1=idx, op=ALU.add))
                link(dve.tensor_reduce(low, cand, AX.X, ALU.min))
                link(dve.tensor_tensor(out=out, in0=cand, in1=low.broadcast_to([P, 3, n]), op=ALU.is_equal))

            def route(L):
                turn(2 * L)
                dve.wait_ge(logits_done, L + 1)
                if L == 0:
                    dve.wait_ge(zeroed, 7)
                link(dve.tensor_copy(lg[:, 0:2, :], ps[:, 5, 0:72].rearrange("p (i n) -> p i n", i=2)))
                link(dve.tensor_copy(lg[0:24, 2, :], ps[0:24, 5, 72:108]))
                grp, gs, eg = lg[:, :, 0:NG], sm[:, 0, :, 0:NG], sm[:, 1, :, 0:NG]
                m, ohg, pg = sm[:, 2, :, 0:1], sm[:, 3, :, 0:NG], sm[:, 4, :, 0:1]
                link(dve.tensor_reduce(m, grp, AX.X, ALU.max))
                dve.tensor_tensor(out=gs, in0=grp, in1=m.broadcast_to([P, 3, NG]), op=ALU.subtract).then_inc(exp_in, 1)
                dve.wait_ge(exp_in, 2 * L + 1)
                first_best(gs, True, ohg)
                link(dve.tensor_tensor(out=le4[:, :, :, :], in0=lg[:, :, NG:NG + NE].rearrange("p i (g e) -> p i e g", g=NG),
                                       in1=ohg.unsqueeze(2).broadcast_to([P, 3, EPG, NG]), op=ALU.mult))
                le, oh1, oh2, d2 = sm[:, 5, :, :], sm[:, 6, :, :], sm[:, 7, :, :], sm[:, 8, :, :]
                link(dve.tensor_reduce(le, le4[:, :, :, :], AX.X, ALU.add))
                m1, m2, e2 = sm[:, 11, :, 0:1], sm[:, 9, :, 0:1], sm[:, 10, :, 0:1]
                link(dve.tensor_reduce(m1, le, AX.X, ALU.max))
                link(dve.tensor_tensor(out=le, in0=le, in1=m1.broadcast_to([P, 3, EPG]), op=ALU.subtract))
                first_best(le, True, oh1)
                link(dve.scalar_tensor_tensor(out=d2, in0=oh1, scalar=-3e38, in1=le, op0=ALU.mult, op1=ALU.add))
                dve.tensor_reduce(m2, d2, AX.X, ALU.max).then_inc(exp_in, 1)
                dve.wait_ge(exp_in, 2 * L + 2)
                link(dve.tensor_tensor(out=d2, in0=d2, in1=m2.broadcast_to([P, 3, EPG]), op=ALU.subtract))
                first_best(d2, True, oh2)
                link(dve.tensor_tensor(out=d2, in0=oh1, in1=oh2, op=ALU.add))

                def spread(out, in8):
                    return dve.tensor_tensor(out=out[:, :, :].rearrange("p i (g e) -> p i g e", g=NG),
                                             in0=ohg.unsqueeze(3).broadcast_to([P, 3, NG, EPG]),
                                             in1=in8.unsqueeze(2).broadcast_to([P, 3, NG, EPG]), op=ALU.mult)
                spread(assign, d2).then_inc(routed, 1)
                dve.wait_ge(routed, L + 1)
                dve.wait_ge(exp_out, 2 * L + 2)
                g1, g2, den = sm[:, 14, :, 0:1], sm[:, 14, :, 1:2], sm[:, 14, :, 2:3]
                link(dve.tensor_reduce(pg, eg, AX.X, ALU.add))
                link(dve.scalar_tensor_tensor(out=den, in0=e2, scalar=1.0, in1=pg, op0=ALU.add, op1=ALU.mult))
                link(dve.reciprocal(g1, den))
                link(dve.tensor_tensor(out=g2, in0=g1, in1=e2, op=ALU.mult))
                link(dve.tensor_tensor(out=oh1, in0=oh1, in1=g1.broadcast_to([P, 3, EPG]), op=ALU.mult))
                link(dve.tensor_tensor(out=oh2, in0=oh2, in1=g2.broadcast_to([P, 3, EPG]), op=ALU.mult))
                link(dve.tensor_tensor(out=oh1, in0=oh1, in1=oh2, op=ALU.add))
                link(spread(gates, oh1))
                dve.wait_ge(placed, L + 1)
                for k, (i0, i1, n) in enumerate(((0, 2, P), (2, 3, 24))):
                    link(dve.scalar_tensor_tensor(
                        out=slot1[0:n, i0:i1, :], in0=ps[0:n, 6, NE * i0:NE * i1].rearrange("p (i e) -> p i e", e=NE),
                        scalar=1.0, in1=assign[0:n, i0:i1, :], op0=ALU.add, op1=ALU.mult))
                link(dve.scalar_tensor_tensor(out=over[:, :, :], in0=slot1[:, :, :], scalar=CAP + 0.5,
                                              in1=gates[:, :, :], op0=ALU.is_gt, op1=ALU.mult))
                link(dve.tensor_reduce(cntf[:, :], ps[0:1, 6, 3 * NE:4 * NE], AX.X, ALU.max))
                dve.tensor_copy(most[:, :], cntf[:, :]).then_inc(most_ready, 1)

            def experts(L):
                dve.wait_ge(residual, 3 * L + 3)
                with dve.Fori(0, LOOPS) as it:
                    for b in range(2):
                        q = NQ * L + b + 1
                        done = it * 2 + q
                        first = dve.snap(it * 8 + 4 * b)
                        rows = lambda t: t[:, :, bass.ds(first, QUAD)].unsqueeze(3).broadcast_to([P, 3, QUAD, CAP])
                        cols = lambda t: t.rearrange("p i (e s) -> p i e s", e=QUAD)
                        dve.tensor_tensor(out=cols(onehot), in0=rows(slot1),
                                          in1=iota1.unsqueeze(1).unsqueeze(1).broadcast_to([P, 3, QUAD, CAP]),
                                          op=ALU.is_equal).then_inc(onehot_ready, 1)
                        dve.wait_ge(onehot_ready, done)
                        dve.tensor_tensor(out=cols(gated), in0=cols(onehot), in1=rows(gates), op=ALU.mult).then_inc(gated_ready, 1)
                        dve.wait_ge(dispatched, it * 4 + 2 * q)
                        dve.tensor_copy(xg[:, 4:8, :], ps[:, 7, :].rearrange("p (k s) -> p k s", k=4)).then_inc(xg_d, 1)
                        dve.wait_ge(gT_turned, done)
                        dve.tensor_copy(gT, ps[:, 4, 0:T]).then_inc(gT_ready, 1)
                        dve.wait_ge(silu_done, done)
                        through = it * (2 * QCHUNKS) + used_up(BASE[L] + QCHUNKS * b - 1)
                        dve.wait_ge(ring_free, through + 8)
                        dve.tensor_tensor(out=h, in0=sil, in1=ps[:, 1, :], op=ALU.mult).then_inc(h_ready, 1)
                        dve.wait_ge(ring_free, through + 12)
                        dve.tensor_copy(ye[:, HALF:D], ps[:, 3, :]).then_inc(ye_d, 1)
                        for j, bank in enumerate((4, 5, 6, 7, 2, 3)):
                            i, k = j // 2, j % 2
                            n = TILES[i][1]
                            dve.wait_ge(combined, it * 12 + (6 * (q - 1) + j + 1))
                            zz = z[0:n, i, HALF * k:HALF * k + HALF]
                            dve.tensor_tensor(out=zz, in0=zz, in1=ps[0:n, bank, :], op=ALU.add).then_inc(added, 1)

            def overflow(L):
                s = fb[L]
                dve.wait_ge(most_ready, L + 1)
                count = dve.value_load(most[0:1, 0:1], min_val=0, max_val=T)
                with dve.If(count > CAP):
                    with dve.Fori(0, NE) as e:
                        ee = dve.snap(e)
                        for i, (t0, tn) in enumerate(TILES):
                            dve.wait_ge(s["silu"], e * 3 + (i + 1))
                            dve.tensor_tensor(out=h[0:tn, :], in0=sil[0:tn, :], in1=ps[0:tn, 1, :], op=ALU.mult).then_inc(s["h"], 1)
                            dve.wait_ge(s["down"], e * 3 + (i + 1))
                            zz = z[0:tn, i, :].rearrange("p (h n) -> p h n", h=2)
                            dve.scalar_tensor_tensor(out=zz, in0=ps[0:tn, 2:4, :], scalar=over[0:tn, i, bass.ds(ee, 1)],
                                                     in1=zz, op0=ALU.mult, op1=ALU.add).then_inc(s["added"], 1)
                    dve.wait_ge(s["added"], 3 * NE)
                dve.wait_ge(added, 6 * NQ * (L + 1))

            dve.wait_ge(w_in, 48)
            dve.tensor_tensor(out=wp, in0=wp, in1=pscale.rearrange("p (g n) -> p g n", g=NPG).unsqueeze(2)
                              .broadcast_to([P, NPG, 2, PGD]), op=ALU.mult).then_inc(wp_scaled, 1)
            for c in range(1, KD, 2):
                dve.wait_ge(diff_done, c + 1)
                if c == 1:
                    dve.wait_ge(chan_turned, 1)
                    dve.tensor_copy(chan[:, :, :], ps[:, 7, 0:KD * R_N].rearrange("p (k r) -> p k r", k=KD)).then_inc(chan_ready, 1)
                dve.tensor_copy(xT[:, c, :], ps[:, c, 0:T]).then_inc(diff_d, 1)
            layer_norm(0)
            dve.wait_ge(vstate_done, 1)
            dve.wait_ge(chan_ready, 1)
            dve.tensor_tensor(out=vstate[:, :, :], in0=ps[:, 7, 0:KD * NSAMP].rearrange("p (k b) -> p k b", k=KD),
                              in1=chan[:, :, R_BDW:R_BDW + 1].broadcast_to([P, KD, NSAMP]), op=ALU.add).then_inc(prep_done, 1)
            route(0)
            experts(0)
            overflow(0)
            layer_norm(1)
            turn(1)
            link(dve.memset(u[:, :, 0:CSTATE], 0.0))
            dve.wait_ge(prep_done, 1)
            link(dve.tensor_copy(v[:, :, NPROMPT:T], vstate[:, :, :]))
            for e in range(KD):
                dve.wait_ge(sig_ready, e + 1)
                dve.scalar_tensor_tensor(out=u[:, e, CSTATE:UW], in0=ps[:, 2 * (e % 4), 0:T], scalar=chan[:, e, R_BA:R_BA + 1],
                                         in1=sg[:, e, :], op0=ALU.add, op1=ALU.mult).then_inc(u_ready, 1)
                dve.wait_ge(u_ready, e + 1)
                link(dve.tensor_scalar(v[:, e, 0:NPROMPT], u[:, e, 0:NPROMPT], chan[:, e, 0:1],
                                       chan[:, e, R_BDW:R_BDW + 1], ALU.mult, ALU.add))
                for j in range(1, TAPS):
                    n = NPROMPT if j < TAPS - 1 else T
                    ins = dve.scalar_tensor_tensor(out=v[:, e, 0:n], in0=u[:, e, j:j + n], scalar=chan[:, e, j:j + 1],
                                                   in1=v[:, e, 0:n], op0=ALU.mult, op1=ALU.add)
                    if j < TAPS - 1:
                        link(ins)
                    else:
                        ins.then_inc(conv_done, 1)
            dve.wait_ge(conv_done, KD)
            dve.wait_ge(mean_done, 1)
            for k in range(2):
                vv = v[:, 4 * k:4 * k + 4, :]
                dve.tensor_tensor(out=vv, in0=vv, in1=ps[:, 0, 0:T].unsqueeze(1).broadcast_to([P, 4, T]),
                                  op=ALU.subtract).then_inc(cent_ready, 1)
            dve.wait_ge(var_done, 1)
            dve.tensor_scalar(rstd[:, :], ps[:, 1, 0:T], EPS, None, ALU.add).then_inc(crt_in, 1)
            dve.wait_ge(crt_out, 1)
            link(dve.reciprocal(rstd[:, :], rstd[:, :]))
            dve.wait_ge(cent_ready, 2)
            for k in range(2):
                vv = v[:, 4 * k:4 * k + 4, :]
                dve.tensor_tensor(out=vv, in0=vv, in1=rstd[:, :].unsqueeze(1).broadcast_to([P, 4, T]),
                                  op=ALU.mult).then_inc(vn_ready, 1)
            for k in range(2):
                dve.wait_ge(urow_turned, k + 1)
                dve.tensor_copy(urow[0:38, HALF * k:HALF * k + HALF], ps[0:38, 6 + k, :]).then_inc(urow_ready, 1)
            layer_norm(2)
            route(1)
            experts(1)
            overflow(1)
            layer_norm(3)

        @block.tensor
        def _(pe):
            def turn(m):
                for i, (t0, tn) in enumerate(TILES):
                    pe.wait_ge(normed, 3 * m + i + 1)
                    for k in range(KD):
                        if i < 2:
                            bank, at = 2 * i + k // 4, (k % 4) * P
                        else:
                            bank, at = 4, k * tn
                        mm = pe.transpose(ps[:, bank, at:at + tn], x[0:tn, i, k * P:(k + 1) * P], ident[0:tn, 0:tn])
                        if k % 4 == 3 and (i < 2 or k == 7):
                            mm.then_inc(turned, 1)

            def have_xT(m):
                pe.wait_ge(xT_a, 3 * (m + 1))
                pe.wait_ge(xT_d, 2 * (m + 1))

            def route(L):
                turn(2 * L)
                have_xT(2 * L)
                if L == 0:
                    pe.wait_ge(prep_in, 16 * 15)
                for i, (t0, tn) in enumerate(TILES):
                    for k in range(KD):
                        mm = pe.matmul(ps[0:tn, 5, 36 * i:36 * i + 36], xT[:, k, t0:t0 + tn], wr[:, L, k, :],
                                       start=(k == 0), stop=(k == KD - 1))
                mm.then_inc(logits_done, 1)
                pe.wait_ge(routed, L + 1)
                for i, (t0, tn) in enumerate(TILES):
                    o = ps[0:tn, 6, NE * i:NE * i + NE]
                    for j in range(i):
                        pe.matmul(o, ones[:, 0:tn], assign[:, j, :], start=(j == 0), stop=False)
                    pe.matmul(o, upper[0:tn, 0:tn], assign[0:tn, i, :], start=(i == 0), stop=True)
                for i, (t0, tn) in enumerate(TILES):
                    mm = pe.matmul(ps[0:1, 6, 3 * NE:4 * NE], ones[0:tn, 0:1], assign[0:tn, i, :],
                                   start=(i == 0), stop=(i == 2))
                mm.then_inc(placed, 1)

            def experts(L):
                with pe.Fori(0, LOOPS) as it:
                    for b in range(2):
                        q = NQ * L + b + 1
                        done = it * 2 + q
                        pe.wait_ge(onehot_ready, done)
                        for k in range(KD):
                            for i, (t0, tn) in enumerate(TILES):
                                mm = pe.matmul(ps[:, 6 + k // 4, (k % 4) * P:(k % 4 + 1) * P], x[0:tn, i, k * P:(k + 1) * P],
                                               onehot[0:tn, i, :], start=(i == 0), stop=(i == 2))
                            if k % 4 == 3:
                                mm.then_inc(dispatched, 1)
                        pe.wait_ge(gated_ready, done)
                        for i, (t0, tn) in enumerate(TILES):
                            mm = pe.transpose(ps[:, 4, t0:t0 + tn], gated[0:tn, i, :], ident[0:tn, 0:tn])
                        mm.then_inc(gT_turned, 1)
                        pe.wait_ge(xg_a, done)
                        pe.wait_ge(xg_d, done)

                        def chunk(c):
                            n = BASE[L] + QCHUNKS * b + c
                            pe.wait_ge(filled[ring_slot(n)], it * 96 + fills(n))
                            return ring[:, ring_slot(n), :]

                        for c in range(8):
                            w = chunk(c).rearrange("p (e k f) -> p e k f", e=QUAD, k=2)
                            for kk in range(2):
                                k = 2 * (c % 4) + kk
                                for e in range(QUAD):
                                    mm = pe.matmul(ps[32 * e:32 * e + 32, c // 4, :], xg[:, k, 32 * e:32 * e + 32],
                                                   w[:, e, kk, :], start=(k == 0), stop=(k == KD - 1))
                            mm.then_inc(ring_free, 1)
                        pe.wait_ge(h_ready, done)
                        for k in range(KF):
                            mm = pe.transpose(ps[:, 5, k * P:(k + 1) * P], h[:, k * P:(k + 1) * P], ident)
                        mm.then_inc(hT_turned, 1)
                        pe.wait_ge(hT_ready, done)
                        for c in range(KF):
                            w = chunk(8 + c).rearrange("p (e f) -> p e f", e=QUAD)
                            for hh in range(2):
                                for e in range(QUAD):
                                    mm = pe.matmul(ps[32 * e:32 * e + 32, 2 + hh, :], hT[:, c, 32 * e:32 * e + 32],
                                                   w[:, e, HALF * hh:HALF * hh + HALF], start=(c == 0), stop=(c == KF - 1))
                            mm.then_inc(ring_free, 1)
                        pe.wait_ge(gT_ready, done)
                        pe.wait_ge(ye_a, done)
                        pe.wait_ge(ye_d, done)
                        for j, bank in enumerate((4, 5, 6, 7, 2, 3)):
                            t0, tn = TILES[j // 2]
                            pe.matmul(ps[0:tn, bank, :], gT[:, t0:t0 + tn], ye[:, HALF * (j % 2):HALF * (j % 2) + HALF],
                                      start=True, stop=True).then_inc(combined, 1)

            def overflow(L):
                s = fb[L]
                pe.wait_ge(most_ready, L + 1)
                count = pe.value_load(most[0:1, 0:1], min_val=0, max_val=T)
                with pe.If(count > CAP):
                    pe.wait_ge(added, 6 * NQ * (L + 1))
                    pe.sem_inc(s["used"], 1)
                    with pe.Fori(0, NE) as e:
                        for i, (t0, tn) in enumerate(TILES):
                            for m in range(2):
                                if i == 0:
                                    pe.wait_ge(s[f"fill{m}"], e * 16 + 16)
                                w = ring[:, m, :].rearrange("p (k f) -> p k f", k=KD)
                                for k in range(KD):
                                    mm = pe.matmul(ps[0:tn, m, :], xT[:, k, t0:t0 + tn], w[:, k, :], start=(k == 0), stop=(k == KD - 1))
                            mm.then_inc(s["hidden"], 1)
                            pe.wait_ge(s["h"], e * 3 + (i + 1))
                            for k in range(KF):
                                mm = pe.transpose(ps[:, 5, k * P:(k + 1) * P], h[:, k * P:(k + 1) * P], ident)
                            mm.then_inc(s["turned"], 1)
                            pe.wait_ge(s["hT"], e * 3 + (i + 1))
                            if i == 0:
                                pe.wait_ge(s["fill2"], e * 16 + 16)
                            w = ring[:, 2, :].rearrange("p (k f) -> p k f", k=KF)
                            for k in range(KF):
                                for hh in range(2):
                                    mm = pe.matmul(ps[0:tn, 2 + hh, :], hT[:, k, 0:tn], w[:, k, HALF * hh:HALF * hh + HALF],
                                                   start=(k == 0), stop=(k == KF - 1))
                            mm.then_inc(s["down"], 1)
                            pe.wait_ge(s["added"], e * 3 + (i + 1))
                        pe.sem_inc(s["used"], 1)

            pe.wait_ge(w_in, 48)
            pe.wait_ge(prep_in, 16 * 15)
            for k in range(KD):
                mm = pe.transpose(ps[:, 7, k * R_N:(k + 1) * R_N], crow[:, k * P:(k + 1) * P], ident[0:R_N, 0:R_N])
            mm.then_inc(chan_turned, 1)
            pe.wait_ge(x_in, 16 * 7)
            band = lambda at, n, g: bands[:, at + g * n:at + (g + 1) * n]
            for c in range(KD):
                g, cols = c // 2, slice(c * P, (c + 1) * P)
                o = ps[:, c, :]
                if c == 7:
                    pe.wait_ge(chan_ready, 1)
                pe.matmul(o[:, 0:144], x[:, 0, cols], band(B_0, 144, g), start=True, stop=False)
                pe.matmul(o[:, 128:144], x[:, 1, cols], band(B_1, 144, g)[:, 0:16], start=False, stop=False)
                pe.matmul(o[:, 144:272], x[:, 1, cols], band(B_1, 144, g)[:, 16:144], start=False, stop=False)
                pe.matmul(o[:, 272:280], pstate[0:120, cols], band(B_S, 8, g)[0:120, :], start=False, stop=False)
                pe.matmul(o[:, 256:280], x[0:24, 2, cols], band(B_2, 24, g)[0:24, :], start=False, stop=True).then_inc(diff_done, 1)
            pe.wait_ge(wp_scaled, 1)
            pe.wait_ge(diff_a, 4)
            pe.wait_ge(diff_d, 4)
            for i, (t0, tn) in enumerate(TILES):
                for g in range(NPG):
                    for k in range(2):
                        mm = pe.matmul(ps[0:tn, 2 * i + g // 2, (g % 2) * PGD:(g % 2 + 1) * PGD], xT[:, 2 * g + k, t0:t0 + tn],
                                       wp[:, g, k, :], start=(k == 0), stop=(k == 1))
                mm.then_inc(pooled, 1)
            pe.wait_ge(state_mul, 2)
            for k in range(KD):
                for hh in range(2):
                    mm = pe.matmul(ps[:, 7, k * 8 + 4 * hh:k * 8 + 4 * hh + 4], cs_raw[0:120, hh, k * P:(k + 1) * P],
                                   cst[0:120, C_SELB:C_SELB + 4], start=True, stop=True)
            mm.then_inc(vstate_done, 1)
            route(0)
            experts(0)
            overflow(0)
            turn(1)
            have_xT(1)
            for e in range(KD):
                n = MIX_BASE + e // 2
                if e % 2 == 0:
                    pe.wait_ge(filled[ring_slot(n)], fills(n))
                w = ring[:, ring_slot(n), :].rearrange("p (k h n) -> p k h n", k=KD, h=2)
                if e >= 4:
                    pe.wait_ge(u_ready, e - 3)
                for hh in range(2):
                    for k in range(KD):
                        mm = pe.matmul(ps[:, 2 * (e % 4) + hh, 0:T], w[:, k, hh, (e % 2) * P:(e % 2 + 1) * P], xT[:, k, :],
                                       start=(k == 0), stop=(k == KD - 1))
                mm.then_inc(ring_free if e % 2 else glu_done, 1)
            pe.wait_ge(u_ready, KD)
            for k in range(KD):
                mm = pe.transpose(ps[0:38, 6 + k // 4, (k % 4) * P:(k % 4 + 1) * P], u[:, k, UW - 38:UW], ident)
                if k % 4 == 3:
                    mm.then_inc(urow_turned, 1)
            for k in range(KD):
                pe.wait_ge(conv_done, k + 1)
                mm = pe.matmul(ps[:, 0, 0:T], mean_w, v[:, k, :], start=(k == 0), stop=(k == KD - 1))
            mm.then_inc(mean_done, 1)
            for k in range(KD):
                pe.wait_ge(sq_ready, k + 1)
                mm = pe.matmul(ps[:, 1, 0:T], mean_w, sq[:, k, :], start=(k == 0), stop=(k == KD - 1))
            mm.then_inc(var_done, 1)
            for i, (t0, tn) in enumerate(TILES):
                for hh in range(2):
                    pe.matmul(ps[0:tn, 2 * i + hh, :], ones[0:1, 0:tn], bpw[:, HALF * hh:HALF * hh + HALF], start=True, stop=False) \
                        if i else None
            pe.wait_ge(vn_ready, 2)
            for hh in range(2):
                pe.matmul(ps[:, hh, :], ones[0:1, :], bpw[:, HALF * hh:HALF * hh + HALF], start=True, stop=False)
            for i, (t0, tn) in enumerate(TILES):
                for k in range(KD):
                    n = MIX_BASE + 4 + k // 4
                    if i == 0:
                        pe.wait_ge(act_ready, k + 1)
                        if k % 4 == 0:
                            pe.wait_ge(filled[ring_slot(n)], fills(n))
                    w = ring[:, ring_slot(n), :].rearrange("p (k n) -> p k n", k=4)
                    for hh in range(2):
                        mm = pe.matmul(ps[0:tn, 2 * i + hh, :], sq[:, k, t0:t0 + tn], w[:, k % 4, HALF * hh:HALF * hh + HALF],
                                       start=False, stop=(k == KD - 1))
                    if i == 2 and k % 4 == 3:
                        mm.then_inc(ring_free, 1)
                if i < 2:
                    mm.then_inc(pw_done, 1)
            route(1)
            experts(1)
            overflow(1)


_INS = ["x_prompt", "x_sample", "state_pool", "state_conv", "meta", "w_pool", "pool_scale", "w_glu", "b_glu", "w_dw",
        "b_dw", "conv_ln_g", "conv_ln_b", "w_pw", "b_pw", "ln_mix_g", "ln_mix_b", "ln_ffn_g", "ln_ffn_b",
        "w_router_group", "w_router_expert", "w_gate", "w_up", "w_down"]
_OUTS = [(1, SEQ, D), (NSAMP, 1, D), (1, 1, PSTATE, D), (1, NSAMP, PSTATE, D), (1, 1, CSTATE, D), (1, NSAMP, CSTATE, D)]


def kernel(**inputs):
    import concourse.bacc as _bacc
    from concourse.bass_utils import run_bass_kernel_spmd as _run

    nc = _bacc.Bacc("TRN2", target_bir_lowering=False, num_devices=1)
    arrays, args = {}, {}
    cst, bands = constants()
    for name, arr in [(n, inputs[n]) for n in _INS] + [("cst", cst), ("bands", bands)]:
        arr = np.ascontiguousarray(arr)
        arrays[f"in_{name}"] = arr
        args[name] = nc.dram_tensor(f"in_{name}", arr.shape, mybir.dt.from_np(arr.dtype), kind="ExternalInput").ap()
    outs = [nc.dram_tensor(f"out_{i}", s, mybir.dt.float32, kind="ExternalOutput").ap() for i, s in enumerate(_OUTS)]
    build(nc, args, outs)
    r = _run(nc, [arrays], core_ids=[0])
    return tuple(r.results[0][f"out_{i}"] for i in range(len(_OUTS)))
```

```python
import concourse.bass as bass
from concourse import mybir
from concourse.alu_op_type import AluOpType as ALU
from contextlib import ExitStack
import numpy as np

D = 1024
F = D // 2
P = 128
KD, KF = D // P, F // P
HALF = 512
META, SEQ, NSAMP = 16, 256, 8
NPROMPT = META + SEQ
T = NPROMPT + NSAMP
TILES = [(0, 128), (128, 128), (256, 24)]
WINDOWS = (2, 4, 8, 16)
NPG, PGD = len(WINDOWS), D // len(WINDOWS)
PSTATE, CSTATE, TAPS = 15, 30, 31
NG, EPG = 4, 8
NE = NG * EPG
QUAD = 4
CAP = P // QUAD
NQ = NE // QUAD
DEPTH = 2
ALPHA = (2.0 * DEPTH) ** 0.25
EPS = 1e-5
CHUNK = 4096
RING = 8
QCHUNKS = 12
LOOPS = NQ // 2
MIX_CHUNKS = 6
BASE = [0, NQ * QCHUNKS + MIX_CHUNKS]
MIX_BASE = NQ * QCHUNKS
BIG = 64.0

C_ID, C_UP, C_ONE, C_IOTA, C_SELB, C_MEAN, C_TIE = 0, 128, 256, 384, 416, 420, 548
C_END = 556
B_0, B_1, B_2, B_S, B_END = 0, 4 * 144, 8 * 144, 8 * 144 + 4 * 24, 8 * 144 + 4 * 24 + 4 * 8
R_BDW, R_G, R_B, R_BA, R_BG, R_N = 31, 32, 33, 34, 35, 36


def constants():
    c = np.zeros((P, C_END), np.float32)
    c[:, C_ID:C_ID + P] = np.eye(P)
    c[:, C_UP:C_UP + P] = np.triu(np.ones((P, P)), 1)
    c[:, C_ONE:C_ONE + P] = 1
    c[:, C_IOTA:C_IOTA + CAP] = np.arange(1, CAP + 1)
    for b in range(4):
        c[b * CSTATE:(b + 1) * CSTATE, C_SELB + b] = 1
    c[:, C_MEAN:C_MEAN + P] = 1.0 / D
    c[:, C_TIE:C_TIE + EPG] = np.arange(EPG) - BIG
    bands = np.zeros((P, B_END), np.float32)
    for g, w in enumerate(WINDOWS):
        for p in range(P):
            for j in range(144):
                for at, off in ((B_0, 0), (B_1, P)):
                    if 0 <= j - p < w:
                        bands[p, at + g * 144 + j] = 1.0 / min(off + j + 1, w)
                    if j == p:
                        bands[p, at + g * 144 + j] -= 1
        for p in range(META):
            for j in range(p, min(p + w, META)):
                bands[p, B_2 + g * 24 + j] = 1.0 / w
            bands[p, B_2 + g * 24 + p] -= 1
        for b in range(NSAMP):
            bands[META + b, B_2 + g * 24 + META + b] = 1.0 / w - 1
            for r in range(PSTATE + 1 - w, PSTATE):
                bands[b * PSTATE + r, B_S + g * 8 + b] = 1.0 / w
    return c, bands


def build(nc, a, outs):
    fp32, i32 = mybir.dt.float32, mybir.dt.int32
    ACT = mybir.ActivationFunctionType
    AX = mybir.AxisListType
    y_prompt, y_sample, pool_p, pool_s, conv_p, conv_s = outs

    ctx = ExitStack()
    with ctx:
        def sb(name, shape, dt=fp32):
            return ctx.enter_context(nc.sbuf_tensor(name, shape, dt))

        def sem(name):
            return ctx.enter_context(nc.semaphore(name))

        ring = sb("ring", [P, RING, CHUNK])
        cst = sb("cst", [P, C_END])
        x = sb("x", [P, 3, D])
        z = sb("z", [P, 3, D])
        xT = sb("xT", [P, KD, T])
        gb = sb("gb", [P, 2, D])
        wr = sb("wr", [P, DEPTH, KD, 36])
        lg = sb("lg", [P, 3, 36])
        st = sb("st", [P, 3, 12])
        mv = sb("mv", [P, 3, 2])
        rs = sb("rs", [P, 3])
        warm = sb("warm", [1, 16])
        sm = sb("sm", [P, 16, 3, 8])
        assign = sb("assign", [P, 3, NE])
        gates = sb("gates", [P, 3, NE])
        slot1 = sb("slot1", [P, 3, NE])
        over = sb("over", [P, 3, NE])
        le4 = sb("le4", [P, 3, EPG, NG])
        cnt = sb("cnt", [1, NE])
        cntf = sb("cntf", [1, 1])
        most = sb("most", [1, 1], i32)
        chan = sb("chan", [P, KD, R_N])
        vstate = sb("vstate", [P, KD, NSAMP])
        bpw = sb("bpw", [1, D])
        U = sb("U", [P, 6144])

        def view(at, n, **k):
            v = U[:, at:at + n]
            return v.rearrange(k.pop("r"), **k) if k else v

        wp = view(0, 2048, r="p (g k n) -> p g k n", g=NPG, k=2)
        cs_raw = view(2048, 2 * D, r="p (h n) -> p h n", h=2)
        wrep = view(2048 + 2 * D, D)
        zflat = z[:, :, :].rearrange("p i n -> p (i n)")
        bands = zflat[:, 0:B_END]
        pstate = zflat[:, B_END:B_END + D]
        crow = view(2048 + 3 * D, D)[0:R_N, :]
        pscale = xT[:, :, :].rearrange("p a b -> p (a b)")[:, 0:D]
        onehot = view(0, 384, r="p (i s) -> p i s", i=3)
        gated = view(384, 384, r="p (i s) -> p i s", i=3)
        gT = view(768, T)
        xg = view(1056, 1024, r="p (k s) -> p k s", k=KD)
        sil = view(2080, F)
        h = view(2592, F)
        hT = view(3104, F, r="p (k s) -> p k s", k=KF)
        ye = view(3616, D)
        UW = CSTATE + T
        u = view(0, KD * UW, r="p (k n) -> p k n", k=KD)
        v = zflat[:, 0:KD * T].rearrange("p (k n) -> p k n", k=KD)
        sq = view(KD * UW, KD * T, r="p (k n) -> p k n", k=KD)
        sg = sq
        urow = view(KD * (UW + T), D)
        NDIAG = 6
        diag = zflat[:, KD * T:KD * T + NDIAG * P].rearrange("p (n c) -> p n c", n=NDIAG)
        rstd = view(KD * (UW + T) + D, T)

        ps = ctx.enter_context(nc.psum_tensor("ps", [P, 8, HALF], fp32))

        ident = cst[:, C_ID:C_ID + P]
        upper = cst[:, C_UP:C_UP + P]
        ones = cst[:, C_ONE:C_ONE + P]
        iota1 = cst[:, C_IOTA:C_IOTA + CAP]
        mean_w = cst[:, C_MEAN:C_MEAN + P]
        tie = cst[:, C_TIE:C_TIE + EPG]

        filled = [sem(f"filled{s}") for s in range(RING)]
        ring_free = sem("ring_free")
        x_in, w_in, prep_in, gb_in = (sem(n) for n in ("x_in", "w_in", "prep_in", "gb_in"))
        outs_done = sem("outs_done")
        zeroed = sem("zeroed")
        wp_scaled = sem("wp_scaled")
        state_mul = sem("state_mul")
        diff_done, diff_a, diff_d, pooled = (sem(n) for n in ("diff_done", "diff_a", "diff_d", "pooled"))
        chan_turned, chan_ready, vstate_done = (sem(n) for n in ("chan_turned", "chan_ready", "vstate_done"))
        prep_done = sem("prep_done")
        chain = sem("chain")
        root_in, root_out, normed, crt_in, crt_out = (
            sem(n) for n in ("root_in", "root_out", "normed", "crt_in", "crt_out"))
        turned, xT_ready = sem("turned"), sem("xT_ready")
        diag_ready, diag_used, conv7_done = sem("diag_ready"), sem("diag_used"), sem("conv7_done")
        logits_done, exp_in, exp_out, routed, placed, slots_ready, most_ready = (
            sem(n) for n in ("logits_done", "exp_in", "exp_out", "routed", "placed", "slots_ready", "most_ready"))
        residual = sem("residual")
        onehot_ready, gated_ready, dispatched, gT_turned, gT_ready, xg_a, xg_d = (
            sem(n) for n in ("onehot_ready", "gated_ready", "dispatched", "gT_turned", "gT_ready", "xg_a", "xg_d"))
        silu_done, h_ready, hT_turned, hT_ready, ye_a, ye_d, combined, added = (
            sem(n) for n in ("silu_done", "h_ready", "hT_turned", "hT_ready", "ye_a", "ye_d", "combined", "added"))
        glu_done, sig_ready, u_ready, conv_step, conv_done = (
            sem(n) for n in ("glu_done", "sig_ready", "u_ready", "conv_step", "conv_done"))
        mean_done, cent_ready, sq_ready, var_done, vn_ready, act_ready, pw_done, urow_turned, urow_ready = (
            sem(n) for n in ("mean_done", "cent_ready", "sq_ready", "var_done", "vn_ready", "act_ready",
                             "pw_done", "urow_turned", "urow_ready"))
        fb = []
        for L in range(DEPTH):
            fb.append({n: sem(f"over{L}_{n}") for n in (
                "fill0", "fill1", "fill2", "used", "hidden", "silu", "h", "turned", "hT", "down", "added")})

        block = ctx.enter_context(nc.Block())

        def ring_slot(n):
            return n % RING

        def fills(n):
            return 32 * (n // RING + 1)

        def used_up(n):
            return RING + n + 1

        @block.sync
        def _(sp):
            mt, xp, xs = a["meta"], a["x_prompt"], a["x_sample"]
            sp.dma_start(x[0:META, 0, :], mt).then_inc(x_in, 16)
            sp.dma_start(x[META:P, 0, :], xp[0, 0:112, :]).then_inc(x_in, 16)
            sp.dma_start(x[:, 1, :], xp[0, 112:240, :]).then_inc(x_in, 16)
            sp.dma_start(x[0:16, 2, :], xp[0, 240:256, :]).then_inc(x_in, 16)
            sp.dma_start(x[16:24, 2, :], xs[:, 0, :]).then_inc(x_in, 16)
            sp.dma_start(pstate[0:120, :], a["state_pool"][0].rearrange("b j d -> (b j) d")).then_inc(x_in, 16)
            sp.dma_start(bands, a["bands"]).then_inc(x_in, 16)
            sp.dma_start(wp, a["w_pool"][0].rearrange("g (k p) n -> p g k n", p=P)).then_inc(w_in, 16)
            sp.dma_start(pscale, a["pool_scale"][0:1, :].broadcast_to([P, D])).then_inc(w_in, 16)
            sp.dma_start(cst[:, :], a["cst"]).then_inc(w_in, 16)
            sp.dma_start(gb[:, 0, :], a["ln_mix_g"][0:1, :].broadcast_to([P, D])).then_inc(gb_in, 16)
            sp.dma_start(gb[:, 1, :], a["ln_mix_b"][0:1, :].broadcast_to([P, D])).then_inc(gb_in, 16)
            sp.dma_start(crow[0:TAPS, :], a["w_dw"][0]).then_inc(prep_in, 16)
            sp.dma_start(crow[R_BDW:R_BDW + 1, :], a["b_dw"]).then_inc(prep_in, 16)
            sp.dma_start(crow[R_G:R_G + 1, :], a["conv_ln_g"]).then_inc(prep_in, 16)
            sp.dma_start(crow[R_B:R_B + 1, :], a["conv_ln_b"]).then_inc(prep_in, 16)
            sp.dma_start(crow[R_BA:R_BG + 1, :], a["b_glu"].rearrange("o (h n) -> (o h) n", h=2)).then_inc(prep_in, 16)
            sp.dma_start(cs_raw[0:120, :, :], a["state_conv"][0].rearrange("(h b) j d -> (b j) h d", h=2)).then_inc(prep_in, 16)
            for b in range(4):
                sp.dma_start(wrep[b * CSTATE:(b + 1) * CSTATE, :], a["w_dw"][0, 0:CSTATE, :]).then_inc(prep_in, 16)
            sp.sem_inc(ring_free, RING)

            def load(n, parts, count=None):
                sp.wait_ge(ring_free, n + 1 if count is None else count)
                for dst, src in parts:
                    sp.dma_start(dst, src).then_inc(filled[ring_slot(n)], 32 // len(parts))

            def experts(L):
                up = [a[w][L].rearrange("e (k p) f -> p e k f", p=P) for w in ("w_gate", "w_up")]
                down = a["w_down"][L].rearrange("e (k p) n -> p e k n", p=P)
                with sp.Fori(0, LOOPS) as it:
                    for b in range(2):
                        first = sp.snap(it * 8 + 4 * b)
                        for c in range(QCHUNKS):
                            n = BASE[L] + QCHUNKS * b + c
                            if c < 8:
                                dst = ring[:, ring_slot(n), :].rearrange("p (e k f) -> p e k f", e=QUAD, k=2)
                                parts = [(dst[:, :, k, :], up[c // 4][:, bass.ds(first, QUAD), 2 * (c % 4) + k, :])
                                         for k in range(2)]
                            else:
                                dst = ring[:, ring_slot(n), :].rearrange("p (e f) -> p e f", e=QUAD)
                                parts = [(dst, down[:, bass.ds(first, QUAD), c - 8, :])]
                            load(n, parts, it * (2 * QCHUNKS) + (n + 1))

            def overflow(L):
                s = fb[L]
                sp.wait_ge(most_ready, L + 1)
                count = sp.value_load(most[0:1, 0:1], min_val=0, max_val=T)
                with sp.If(count > CAP):
                    sp.wait_ge(ring_free, RING + BASE[L] + NQ * QCHUNKS)
                    with sp.Fori(0, NE) as e:
                        ee = sp.snap(e)
                        for m, w in enumerate(("w_gate", "w_up", "w_down")):
                            kk = 4 if m == 2 else 8
                            src = a[w][L][bass.ds(ee, 1), :, :].rearrange("o (k p) f -> p (o k) f", p=P)
                            dst = ring[:, m, :].rearrange("p (k f) -> p k f", k=kk)
                            sp.wait_ge(s["used"], e + 1)
                            sp.dma_start(dst, src).then_inc(s[f"fill{m}"], 16)
                    sp.wait_ge(s["used"], NE + 1)

            experts(0)
            overflow(0)
            glu = a["w_glu"][0].rearrange("(k p) (h n) -> p k h n", p=P, h=2)
            for j in range(4):
                n = MIX_BASE + j
                dst = ring[:, ring_slot(n), :].rearrange("p (k h n) -> p k h n", k=KD, h=2)
                load(n, [(dst[:, :, hh, :], glu[:, :, hh, 256 * j:256 * j + 256]) for hh in range(2)])
            for j in range(2):
                n = MIX_BASE + 4 + j
                load(n, [(ring[:, ring_slot(n), :].rearrange("p (k n) -> p k n", k=4),
                          a["w_pw"][0, 512 * j:512 * j + 512, :].rearrange("(k p) n -> p k n", p=P))])
            experts(1)
            overflow(1)
            sp.wait_ge(normed, 10)
            sp.dma_start(y_prompt[0, 0:112, :], x[META:P, 0, :]).then_inc(outs_done, 16)
            sp.wait_ge(normed, 11)
            sp.dma_start(y_prompt[0, 112:240, :], x[:, 1, :]).then_inc(outs_done, 16)
            sp.wait_ge(normed, 12)
            sp.dma_start(y_prompt[0, 240:256, :], x[0:16, 2, :]).then_inc(outs_done, 16)
            sp.dma_start(y_sample[:, 0, :], x[16:24, 2, :]).then_inc(outs_done, 16)
            sp.wait_ge(outs_done, 16 * 10)

        @block.gpsimd
        def _(pool):
            for t in (lg, assign, gates, slot1, over, sm):
                pool.memset(t[:], 0.0).then_inc(zeroed, 1)
            pool.memset(warm[:], 1.0).then_inc(zeroed, 1)
            pool.wait_ge(prep_in, 16 * 15)
            for hh in range(2):
                pool.tensor_tensor(out=cs_raw[0:120, hh, :], in0=cs_raw[0:120, hh, :], in1=wrep[0:120, :],
                                   op=ALU.mult).then_inc(state_mul, 1)

        @block.scalar
        def _(act):
            for L in range(DEPTH):
                act.dma_start(wr[:, L, :, 0:NG], a["w_router_group"][L].rearrange("(k p) n -> p k n", p=P)).then_inc(prep_in, 16)
                act.dma_start(wr[:, L, :, NG:NG + NE], a["w_router_expert"][L].rearrange("(k p) n -> p k n", p=P)).then_inc(prep_in, 16)
            act.dma_start(bpw[:, :], a["b_pw"]).then_inc(prep_in, 16)
            act.dma_start(pool_p[0, 0], a["x_prompt"][0, SEQ - PSTATE:SEQ, :]).then_inc(outs_done, 16)
            act.dma_start(pool_s[0, :, 0:PSTATE - 1, :], a["state_pool"][0, :, 1:PSTATE, :]).then_inc(outs_done, 16)
            act.dma_start(pool_s[0, :, PSTATE - 1, :], a["x_sample"][:, 0, :]).then_inc(outs_done, 16)
            act.dma_start(conv_s[0, :, 0:CSTATE - 1, :], a["state_conv"][0, :, 1:CSTATE, :]).then_inc(outs_done, 16)

            def load_gb(n):
                g, b = (("ln_mix_g", "ln_mix_b"), ("ln_ffn_g", "ln_ffn_b"))[n % 2]
                L = n // 2
                act.wait_ge(normed, 3 * n)
                act.dma_start(gb[:, 0, :], a[g][L:L + 1, :].broadcast_to([P, D])).then_inc(gb_in, 16)
                act.dma_start(gb[:, 1, :], a[b][L:L + 1, :].broadcast_to([P, D])).then_inc(gb_in, 16)

            preloads = [0]

            def preload(func):
                preloads[0] += 1
                act.activation(warm[:, preloads[0]:preloads[0] + 1], warm[:, 0:1], func)

            def root(n, i):
                tn = TILES[i][1]
                act.wait_ge(root_in, 3 * n + i + 1)
                act.activation(mv[0:tn, i, 1:2], mv[0:tn, i, 1:2], ACT.Sqrt).then_inc(root_out, 1)

            def turn(m, i):
                t0, tn = TILES[i]
                for k in range(2 if i < 2 else 1):
                    act.wait_ge(turned, 5 * m + 2 * i + k + 1)
                    if i < 2:
                        act.activation(xT[:, 4 * k:4 * k + 4, t0:t0 + tn], ps[:, 2 * i + k, :].rearrange("p (k t) -> p k t", k=4),
                                       ACT.Copy).then_inc(xT_ready, 1)
                    else:
                        act.activation(xT[:, :, t0:t0 + tn], ps[:, 4, 0:KD * tn].rearrange("p (k t) -> p k t", k=KD),
                                       ACT.Copy).then_inc(xT_ready, 1)

            def norm_route(L):
                n, m = 2 * L, 2 * L
                root(n, 0)
                root(n, 1)
                turn(m, 0)
                root(n, 2)
                preload(ACT.Exp)
                if L == 0:
                    load_gb(1)
                turn(m, 1)
                turn(m, 2)
                for k in range(2):
                    act.wait_ge(exp_in, 2 * L + k + 1)
                    t = sm[:, 0, :, 0:NG] if k == 0 else sm[:, 9, :, 0:1]
                    o = sm[:, 1, :, 0:NG] if k == 0 else sm[:, 10, :, 0:1]
                    act.activation(o, t, ACT.Exp).then_inc(exp_out, 1)
                act.wait_ge(normed, 6 * L + 3)
                for i, (t0, tn) in enumerate(TILES):
                    act.activation(z[0:tn, i, :], x[0:tn, i, :], ACT.Copy, scale=ALPHA).then_inc(residual, 1)
                preload(ACT.Silu)

            def experts(L):
                with act.Fori(0, LOOPS) as it:
                    for b in range(2):
                        q = NQ * L + b + 1
                        done = it * 2 + q
                        act.wait_ge(dispatched, it * 4 + (2 * q - 1))
                        act.activation(xg[:, 0:4, :], ps[:, 6, :].rearrange("p (k s) -> p k s", k=4), ACT.Copy).then_inc(xg_a, 1)
                        through = it * (2 * QCHUNKS) + used_up(BASE[L] + QCHUNKS * b - 1)
                        act.wait_ge(ring_free, through + 4)
                        act.activation(sil, ps[:, 0, :], ACT.Silu).then_inc(silu_done, 1)
                        act.wait_ge(hT_turned, done)
                        act.activation(hT, ps[:, 5, :].rearrange("p (k s) -> p k s", k=KF), ACT.Copy).then_inc(hT_ready, 1)
                        act.wait_ge(ring_free, through + 12)
                        act.activation(ye[:, 0:HALF], ps[:, 2, :], ACT.Copy).then_inc(ye_a, 1)

            def overflow(L):
                s = fb[L]
                act.wait_ge(most_ready, L + 1)
                count = act.value_load(most[0:1, 0:1], min_val=0, max_val=T)
                with act.If(count > CAP):
                    with act.Fori(0, NE) as e:
                        for i, (t0, tn) in enumerate(TILES):
                            act.wait_ge(s["hidden"], e * 3 + (i + 1))
                            act.activation(sil[0:tn, :], ps[0:tn, 0, :], ACT.Silu).then_inc(s["silu"], 1)
                            act.wait_ge(s["turned"], e * 3 + (i + 1))
                            act.activation(hT, ps[:, 5, :].rearrange("p (k s) -> p k s", k=KF), ACT.Copy).then_inc(s["hT"], 1)

            act.wait_ge(zeroed, 7)
            preload(ACT.Sqrt)
            for c in range(0, KD, 2):
                act.wait_ge(diff_done, c + 1)
                if c == 0:
                    act.wait_ge(wp_scaled, 1)
                act.activation(xT[:, c, :], ps[:, c, 0:T], ACT.Copy).then_inc(diff_a, 1)
            norm_route(0)
            experts(0)
            overflow(0)
            preload(ACT.Sqrt)
            for i in range(3):
                root(1, i)
            preload(ACT.Sigmoid)
            for i in range(3):
                turn(1, i)
            load_gb(2)
            for e in range(KD):
                if e % 2:
                    act.wait_ge(ring_free, used_up(MIX_BASE + e // 2))
                else:
                    act.wait_ge(glu_done, e // 2 + 1)
                act.activation(sg[:, e, :], ps[:, 2 * (e % 4) + 1, 0:T], ACT.Sigmoid,
                               bias=chan[:, e, R_BG:R_BG + 1]).then_inc(sig_ready, 1)
            for j in range(TAPS):
                if j >= NDIAG:
                    act.wait_ge(diag_used, j - NDIAG + 1)
                act.activation(diag[:, j % NDIAG, :], ident, ACT.Copy, scale=chan[:, KD - 1, j:j + 1]).then_inc(diag_ready, 1)
            for k in range(2):
                act.wait_ge(urow_turned, k + 1)
                act.activation(urow[0:38, HALF * k:HALF * k + HALF], ps[0:38, 6 + k, :], ACT.Copy).then_inc(urow_ready, 1)
            act.wait_ge(urow_ready, 2)
            act.dma_start(conv_p[0, 0], urow[0:CSTATE, :]).then_inc(outs_done, 16)
            act.dma_start(conv_s[0, :, CSTATE - 1, :], urow[CSTATE:CSTATE + NSAMP, :]).then_inc(outs_done, 16)
            preload(ACT.Sqrt)
            for e in range(KD):
                act.wait_ge(cent_ready, e // 4 + 1)
                act.activation(sq[:, e, :], v[:, e, :], ACT.Square).then_inc(sq_ready, 1)
            act.wait_ge(crt_in, 1)
            act.activation(rstd, rstd, ACT.Sqrt).then_inc(crt_out, 1)
            preload(ACT.Silu)
            for e in range(KD):
                act.wait_ge(vn_ready, e // 4 + 1)
                act.activation(sq[:, e, :], v[:, e, :], ACT.Silu, bias=chan[:, e, R_B:R_B + 1],
                               scale=chan[:, e, R_G:R_G + 1]).then_inc(act_ready, 1)
            preload(ACT.Sqrt)
            act.wait_ge(outs_done, 16 * 6)
            norm_route(1)
            load_gb(3)
            experts(1)
            overflow(1)
            preload(ACT.Sqrt)
            for i in range(3):
                root(3, i)

        @block.vector
        def _(dve):
            steps = [0]

            def link(ins):
                steps[0] += 1
                ins.then_inc(chain, 1)
                dve.wait_ge(chain, steps[0])

            def stats(i):
                tn = TILES[i][1]
                for k in range(2):
                    ins = dve.bn_stats(st[0:tn, i, 6 * k:6 * k + 6], z[0:tn, i, HALF * k:HALF * k + HALF])
                link(ins)
                link(dve.bn_aggr(mv[0:tn, i, :], st[0:tn, i, :]))
                dve.tensor_scalar(mv[0:tn, i, 1:2], mv[0:tn, i, 1:2], EPS, None, ALU.add).then_inc(root_in, 1)

            def normalise(n, i):
                tn = TILES[i][1]
                if i == 0:
                    dve.wait_ge(gb_in, 32 * (n + 1))
                dve.scalar_tensor_tensor(out=z[0:tn, i, :], in0=z[0:tn, i, :], scalar=mv[0:tn, i, 0:1], in1=gb[0:tn, 0, :],
                                         op0=ALU.subtract, op1=ALU.mult)
                dve.wait_ge(root_out, 3 * n + i + 1)
                link(dve.reciprocal(rs[0:tn, i:i + 1], mv[0:tn, i, 1:2]))
                dve.scalar_tensor_tensor(out=x[0:tn, i, :], in0=z[0:tn, i, :], scalar=rs[0:tn, i:i + 1], in1=gb[0:tn, 1, :],
                                         op0=ALU.mult, op1=ALU.add).then_inc(normed, 1)

            def layer_norm(n):
                if n % 2 == 0:
                    for i in range(3):
                        (residual_pw if n else residual_pool)(i)
                        stats(i)
                        normalise(n, i)
                else:
                    stats(0)
                    stats(1)
                    normalise(n, 0)
                    stats(2)
                    normalise(n, 1)
                    normalise(n, 2)

            def residual_pool(i):
                t0, tn = TILES[i]
                dve.wait_ge(pooled, i + 1)
                link(dve.scalar_tensor_tensor(out=z[0:tn, i, :].rearrange("p (h n) -> p h n", h=2),
                                              in0=x[0:tn, i, :].rearrange("p (h n) -> p h n", h=2), scalar=ALPHA,
                                              in1=ps[0:tn, 2 * i:2 * i + 2, :], op0=ALU.mult, op1=ALU.add))

            def residual_pw(i):
                t0, tn = TILES[i]
                if i < 2:
                    dve.wait_ge(pw_done, i + 1)
                else:
                    dve.wait_ge(ring_free, used_up(MIX_BASE + MIX_CHUNKS - 1))
                if i < 2:
                    ins = dve.scalar_tensor_tensor(out=z[0:tn, i, :].rearrange("p (h n) -> p h n", h=2),
                                                   in0=x[0:tn, i, :].rearrange("p (h n) -> p h n", h=2), scalar=ALPHA,
                                                   in1=ps[0:tn, 2 * i:2 * i + 2, :], op0=ALU.mult, op1=ALU.add)
                else:
                    for hh in range(2):
                        cols = slice(HALF * hh, HALF * hh + HALF)
                        ins = dve.scalar_tensor_tensor(out=z[0:tn, i, cols], in0=x[0:tn, i, cols], scalar=ALPHA,
                                                       in1=ps[32 * hh:32 * hh + tn, 4 + hh, :], op0=ALU.mult, op1=ALU.add)
                link(ins)

            def first_best(val, out):
                n = val.shape[2]
                cand, low = sm[:, 12, :, 0:n], sm[:, 13, :, 0:1]
                link(dve.scalar_tensor_tensor(out=cand, in0=val, scalar=0.0, in1=tie[:, 0:n].unsqueeze(1).broadcast_to([P, 3, n]),
                                              op0=ALU.is_equal, op1=ALU.mult))
                link(dve.tensor_reduce(low, cand, AX.X, ALU.min))
                link(dve.tensor_tensor(out=out, in0=cand, in1=low.broadcast_to([P, 3, n]), op=ALU.is_equal))

            def route(L):
                dve.wait_ge(logits_done, L + 1)
                if L == 0:
                    dve.wait_ge(zeroed, 7)
                link(dve.tensor_copy(lg[:, 0:2, :], ps[:, 6, 0:72].rearrange("p (i n) -> p i n", i=2)))
                link(dve.tensor_copy(lg[0:24, 2, :], ps[0:24, 6, 72:108]))
                grp, gs, eg = lg[:, :, 0:NG], sm[:, 0, :, 0:NG], sm[:, 1, :, 0:NG]
                m, ohg, pg = sm[:, 2, :, 0:1], sm[:, 3, :, 0:NG], sm[:, 4, :, 0:1]
                link(dve.tensor_reduce(m, grp, AX.X, ALU.max))
                dve.tensor_tensor(out=gs, in0=grp, in1=m.broadcast_to([P, 3, NG]), op=ALU.subtract).then_inc(exp_in, 1)
                dve.wait_ge(exp_in, 2 * L + 1)
                first_best(gs, ohg)
                link(dve.tensor_tensor(out=le4[:, :, :, :], in0=lg[:, :, NG:NG + NE].rearrange("p i (g e) -> p i e g", g=NG),
                                       in1=ohg.unsqueeze(2).broadcast_to([P, 3, EPG, NG]), op=ALU.mult))
                le, oh1, oh2, d2 = sm[:, 5, :, :], sm[:, 6, :, :], sm[:, 7, :, :], sm[:, 8, :, :]
                link(dve.tensor_reduce(le, le4[:, :, :, :], AX.X, ALU.add))
                m1, m2, e2 = sm[:, 11, :, 0:1], sm[:, 9, :, 0:1], sm[:, 10, :, 0:1]
                link(dve.tensor_reduce(m1, le, AX.X, ALU.max))
                link(dve.tensor_tensor(out=le, in0=le, in1=m1.broadcast_to([P, 3, EPG]), op=ALU.subtract))
                first_best(le, oh1)
                link(dve.scalar_tensor_tensor(out=d2, in0=oh1, scalar=-3e38, in1=le, op0=ALU.mult, op1=ALU.add))
                dve.tensor_reduce(m2, d2, AX.X, ALU.max).then_inc(exp_in, 1)
                dve.wait_ge(exp_in, 2 * L + 2)
                link(dve.tensor_tensor(out=d2, in0=d2, in1=m2.broadcast_to([P, 3, EPG]), op=ALU.subtract))
                first_best(d2, oh2)
                link(dve.tensor_tensor(out=d2, in0=oh1, in1=oh2, op=ALU.add))

                def spread(out, in8):
                    return dve.tensor_tensor(out=out[:, :, :].rearrange("p i (g e) -> p i g e", g=NG),
                                             in0=ohg.unsqueeze(3).broadcast_to([P, 3, NG, EPG]),
                                             in1=in8.unsqueeze(2).broadcast_to([P, 3, NG, EPG]), op=ALU.mult)
                spread(assign, d2).then_inc(routed, 1)
                dve.wait_ge(routed, L + 1)
                dve.wait_ge(exp_out, 2 * L + 2)
                g1, g2, den = sm[:, 14, :, 0:1], sm[:, 14, :, 1:2], sm[:, 14, :, 2:3]
                link(dve.tensor_reduce(pg, eg, AX.X, ALU.add))
                link(dve.scalar_tensor_tensor(out=den, in0=e2, scalar=1.0, in1=pg, op0=ALU.add, op1=ALU.mult))
                link(dve.reciprocal(g1, den))
                link(dve.tensor_tensor(out=g2, in0=g1, in1=e2, op=ALU.mult))
                link(dve.tensor_tensor(out=oh1, in0=oh1, in1=g1.broadcast_to([P, 3, EPG]), op=ALU.mult))
                link(dve.tensor_tensor(out=oh2, in0=oh2, in1=g2.broadcast_to([P, 3, EPG]), op=ALU.mult))
                link(dve.tensor_tensor(out=oh1, in0=oh1, in1=oh2, op=ALU.add))
                link(spread(gates, oh1))
                dve.wait_ge(placed, L + 1)
                for k, (i0, i1, n) in enumerate(((0, 2, P), (2, 3, 24))):
                    link(dve.scalar_tensor_tensor(
                        out=slot1[0:n, i0:i1, :], in0=ps[0:n, 5, NE * i0:NE * i1].rearrange("p (i e) -> p i e", e=NE),
                        scalar=1.0, in1=assign[0:n, i0:i1, :], op0=ALU.add, op1=ALU.mult))
                link(dve.scalar_tensor_tensor(out=over[:, :, :], in0=slot1[:, :, :], scalar=CAP + 0.5,
                                              in1=gates[:, :, :], op0=ALU.is_gt, op1=ALU.mult))
                link(dve.tensor_reduce(cntf[:, :], ps[0:1, 5, 3 * NE:4 * NE], AX.X, ALU.max))
                dve.tensor_copy(most[:, :], cntf[:, :]).then_inc(most_ready, 1)

            def experts(L):
                dve.wait_ge(residual, 3 * L + 3)
                with dve.Fori(0, LOOPS) as it:
                    for b in range(2):
                        q = NQ * L + b + 1
                        done = it * 2 + q
                        first = dve.snap(it * 8 + 4 * b)
                        rows = lambda t: t[:, :, bass.ds(first, QUAD)].unsqueeze(3).broadcast_to([P, 3, QUAD, CAP])
                        cols = lambda t: t.rearrange("p i (e s) -> p i e s", e=QUAD)
                        dve.tensor_tensor(out=cols(onehot), in0=rows(slot1),
                                          in1=iota1.unsqueeze(1).unsqueeze(1).broadcast_to([P, 3, QUAD, CAP]),
                                          op=ALU.is_equal).then_inc(onehot_ready, 1)
                        dve.wait_ge(onehot_ready, done)
                        dve.tensor_tensor(out=cols(gated), in0=cols(onehot), in1=rows(gates), op=ALU.mult).then_inc(gated_ready, 1)
                        dve.wait_ge(dispatched, it * 4 + 2 * q)
                        dve.tensor_copy(xg[:, 4:8, :], ps[:, 7, :].rearrange("p (k s) -> p k s", k=4)).then_inc(xg_d, 1)
                        dve.wait_ge(gT_turned, done)
                        dve.tensor_copy(gT, ps[:, 4, 0:T]).then_inc(gT_ready, 1)
                        dve.wait_ge(silu_done, done)
                        through = it * (2 * QCHUNKS) + used_up(BASE[L] + QCHUNKS * b - 1)
                        dve.wait_ge(ring_free, through + 8)
                        dve.tensor_tensor(out=h, in0=sil, in1=ps[:, 1, :], op=ALU.mult).then_inc(h_ready, 1)
                        dve.wait_ge(ring_free, through + 12)
                        dve.tensor_copy(ye[:, HALF:D], ps[:, 3, :]).then_inc(ye_d, 1)
                        for j, bank in enumerate((4, 5, 6, 7, 2, 3)):
                            i, k = j // 2, j % 2
                            n = TILES[i][1]
                            dve.wait_ge(combined, it * 12 + (6 * (q - 1) + j + 1))
                            zz = z[0:n, i, HALF * k:HALF * k + HALF]
                            dve.tensor_tensor(out=zz, in0=zz, in1=ps[0:n, bank, :], op=ALU.add).then_inc(added, 1)

            def overflow(L):
                s = fb[L]
                dve.wait_ge(most_ready, L + 1)
                count = dve.value_load(most[0:1, 0:1], min_val=0, max_val=T)
                with dve.If(count > CAP):
                    with dve.Fori(0, NE) as e:
                        ee = dve.snap(e)
                        for i, (t0, tn) in enumerate(TILES):
                            dve.wait_ge(s["silu"], e * 3 + (i + 1))
                            dve.tensor_tensor(out=h[0:tn, :], in0=sil[0:tn, :], in1=ps[0:tn, 1, :], op=ALU.mult).then_inc(s["h"], 1)
                            dve.wait_ge(s["down"], e * 3 + (i + 1))
                            zz = z[0:tn, i, :].rearrange("p (h n) -> p h n", h=2)
                            dve.scalar_tensor_tensor(out=zz, in0=ps[0:tn, 2:4, :], scalar=over[0:tn, i, bass.ds(ee, 1)],
                                                     in1=zz, op0=ALU.mult, op1=ALU.add).then_inc(s["added"], 1)
                    dve.wait_ge(s["added"], 3 * NE)
                dve.wait_ge(added, 6 * NQ * (L + 1))

            dve.wait_ge(w_in, 48)
            dve.tensor_tensor(out=wp, in0=wp, in1=pscale.rearrange("p (g n) -> p g n", g=NPG).unsqueeze(2)
                              .broadcast_to([P, NPG, 2, PGD]), op=ALU.mult).then_inc(wp_scaled, 1)
            for c in range(1, KD, 2):
                dve.wait_ge(diff_done, c + 1)
                if c == 1:
                    dve.wait_ge(wp_scaled, 1)
                dve.tensor_copy(xT[:, c, :], ps[:, c, 0:T]).then_inc(diff_d, 1)
            layer_norm(0)
            route(0)
            dve.wait_ge(chan_turned, 1)
            link(dve.tensor_copy(chan[:, :, :], ps[:, 7, 0:KD * R_N].rearrange("p (k r) -> p k r", k=KD)))
            dve.wait_ge(vstate_done, 1)
            dve.tensor_tensor(out=vstate[:, :, :], in0=ps[:, 7, KD * R_N:KD * R_N + KD * NSAMP].rearrange("p (k b) -> p k b", k=KD),
                              in1=chan[:, :, R_BDW:R_BDW + 1].broadcast_to([P, KD, NSAMP]), op=ALU.add).then_inc(prep_done, 1)
            experts(0)
            overflow(0)
            layer_norm(1)
            link(dve.memset(u[:, :, 0:CSTATE], 0.0))
            dve.wait_ge(prep_done, 1)
            link(dve.tensor_copy(v[:, 0:KD - 1, NPROMPT:T], vstate[:, 0:KD - 1, :]))

            def glu(e):
                dve.wait_ge(sig_ready, e + 1)
                dve.scalar_tensor_tensor(out=u[:, e, CSTATE:UW], in0=ps[:, 2 * (e % 4), 0:T], scalar=chan[:, e, R_BA:R_BA + 1],
                                         in1=sg[:, e, :], op0=ALU.add, op1=ALU.mult).then_inc(u_ready, 1)

            taps = [0]

            def depthwise(slices):
                dve.wait_ge(u_ready, slices[-1] + 1)
                for j in range(TAPS):
                    for e in slices:
                        taps[0] += 1
                        if j:
                            dve.wait_ge(conv_step, taps[0] - len(slices))
                        if j == 0:
                            ins = dve.tensor_scalar(v[:, e, 0:NPROMPT], u[:, e, 0:NPROMPT], chan[:, e, 0:1],
                                                    chan[:, e, R_BDW:R_BDW + 1], ALU.mult, ALU.add)
                        else:
                            n = NPROMPT if j < TAPS - 1 else T
                            ins = dve.scalar_tensor_tensor(out=v[:, e, 0:n], in0=u[:, e, j:j + n], scalar=chan[:, e, j:j + 1],
                                                           in1=v[:, e, 0:n], op0=ALU.mult, op1=ALU.add)
                        ins.then_inc(conv_step, 1)

            glu(0)
            depthwise([0])
            for e in (1, 3, 5):
                glu(e)
                glu(e + 1)
                if e == 5:
                    glu(7)
                depthwise([e, e + 1])
            dve.wait_ge(conv7_done, 1)
            dve.tensor_scalar(v[:, KD - 1, 0:NPROMPT], ps[:, 0, 0:NPROMPT], chan[:, KD - 1, R_BDW:R_BDW + 1], None, ALU.add)
            link(dve.tensor_tensor(out=v[:, KD - 1, NPROMPT:T], in0=ps[:, 0, NPROMPT:T], in1=vstate[:, KD - 1, :], op=ALU.add))
            dve.sem_inc(conv_done, 1)
            dve.wait_ge(mean_done, 1)
            for k in range(2):
                vv = v[:, 4 * k:4 * k + 4, :]
                dve.tensor_tensor(out=vv, in0=vv, in1=ps[:, 1, 0:T].unsqueeze(1).broadcast_to([P, 4, T]),
                                  op=ALU.subtract).then_inc(cent_ready, 1)
            dve.wait_ge(var_done, 1)
            dve.tensor_scalar(rstd, ps[:, 6, 0:T], EPS, None, ALU.add).then_inc(crt_in, 1)
            dve.wait_ge(crt_out, 1)
            link(dve.reciprocal(rstd, rstd))
            dve.wait_ge(cent_ready, 2)
            for k in range(2):
                vv = v[:, 4 * k:4 * k + 4, :]
                dve.tensor_tensor(out=vv, in0=vv, in1=rstd.unsqueeze(1).broadcast_to([P, 4, T]),
                                  op=ALU.mult).then_inc(vn_ready, 1)
            layer_norm(2)
            route(1)
            experts(1)
            overflow(1)
            layer_norm(3)

        @block.tensor
        def _(pe):
            def turn(m, i):
                t0, tn = TILES[i]
                pe.wait_ge(normed, 3 * m + i + 1)
                for k in range(KD):
                    if i < 2:
                        bank, at = 2 * i + k // 4, (k % 4) * P
                    else:
                        bank, at = 4, k * tn
                    mm = pe.transpose(ps[:, bank, at:at + tn], x[0:tn, i, k * P:(k + 1) * P], ident[0:tn, 0:tn])
                    if k % 4 == 3 and (i < 2 or k == 7):
                        mm.then_inc(turned, 1)

            def have_xT(m, i):
                pe.wait_ge(xT_ready, 5 * m + (2, 4, 5)[i])

            def logits(L, i):
                t0, tn = TILES[i]
                have_xT(2 * L, i)
                for k in range(KD):
                    mm = pe.matmul(ps[0:tn, 6, 36 * i:36 * i + 36], xT[:, k, t0:t0 + tn], wr[:, L, k, :],
                                   start=(k == 0), stop=(k == KD - 1))
                if i == 2:
                    mm.then_inc(logits_done, 1)

            def place(L):
                pe.wait_ge(routed, L + 1)
                for i, (t0, tn) in enumerate(TILES):
                    o = ps[0:tn, 5, NE * i:NE * i + NE]
                    for j in range(i):
                        pe.matmul(o, ones[:, 0:tn], assign[:, j, :], start=(j == 0), stop=False)
                    pe.matmul(o, upper[0:tn, 0:tn], assign[0:tn, i, :], start=(i == 0), stop=True)
                for i, (t0, tn) in enumerate(TILES):
                    mm = pe.matmul(ps[0:1, 5, 3 * NE:4 * NE], ones[0:tn, 0:1], assign[0:tn, i, :],
                                   start=(i == 0), stop=(i == 2))
                mm.then_inc(placed, 1)

            def experts(L):
                with pe.Fori(0, LOOPS) as it:
                    for b in range(2):
                        q = NQ * L + b + 1
                        done = it * 2 + q
                        pe.wait_ge(onehot_ready, done)
                        for k in range(KD):
                            for i, (t0, tn) in enumerate(TILES):
                                mm = pe.matmul(ps[:, 6 + k // 4, (k % 4) * P:(k % 4 + 1) * P], x[0:tn, i, k * P:(k + 1) * P],
                                               onehot[0:tn, i, :], start=(i == 0), stop=(i == 2))
                            if k % 4 == 3:
                                mm.then_inc(dispatched, 1)
                        pe.wait_ge(gated_ready, done)
                        for i, (t0, tn) in enumerate(TILES):
                            mm = pe.transpose(ps[:, 4, t0:t0 + tn], gated[0:tn, i, :], ident[0:tn, 0:tn])
                        mm.then_inc(gT_turned, 1)
                        pe.wait_ge(xg_a, done)
                        pe.wait_ge(xg_d, done)

                        def chunk(c):
                            n = BASE[L] + QCHUNKS * b + c
                            pe.wait_ge(filled[ring_slot(n)], it * 96 + fills(n))
                            return ring[:, ring_slot(n), :]

                        for c in range(8):
                            w = chunk(c).rearrange("p (e k f) -> p e k f", e=QUAD, k=2)
                            for kk in range(2):
                                k = 2 * (c % 4) + kk
                                for e in range(QUAD):
                                    mm = pe.matmul(ps[32 * e:32 * e + 32, c // 4, :], xg[:, k, 32 * e:32 * e + 32],
                                                   w[:, e, kk, :], start=(k == 0), stop=(k == KD - 1))
                            mm.then_inc(ring_free, 1)
                        pe.wait_ge(h_ready, done)
                        for k in range(KF):
                            mm = pe.transpose(ps[:, 5, k * P:(k + 1) * P], h[:, k * P:(k + 1) * P], ident)
                        mm.then_inc(hT_turned, 1)
                        pe.wait_ge(hT_ready, done)
                        for c in range(KF):
                            w = chunk(8 + c).rearrange("p (e f) -> p e f", e=QUAD)
                            for hh in range(2):
                                for e in range(QUAD):
                                    mm = pe.matmul(ps[32 * e:32 * e + 32, 2 + hh, :], hT[:, c, 32 * e:32 * e + 32],
                                                   w[:, e, HALF * hh:HALF * hh + HALF], start=(c == 0), stop=(c == KF - 1))
                            mm.then_inc(ring_free, 1)
                        pe.wait_ge(gT_ready, done)
                        pe.wait_ge(ye_a, done)
                        pe.wait_ge(ye_d, done)
                        for j, bank in enumerate((4, 5, 6, 7, 2, 3)):
                            t0, tn = TILES[j // 2]
                            pe.matmul(ps[0:tn, bank, :], gT[:, t0:t0 + tn], ye[:, HALF * (j % 2):HALF * (j % 2) + HALF],
                                      start=True, stop=True).then_inc(combined, 1)

            def overflow(L):
                s = fb[L]
                pe.wait_ge(most_ready, L + 1)
                count = pe.value_load(most[0:1, 0:1], min_val=0, max_val=T)
                with pe.If(count > CAP):
                    pe.wait_ge(added, 6 * NQ * (L + 1))
                    pe.sem_inc(s["used"], 1)
                    with pe.Fori(0, NE) as e:
                        for i, (t0, tn) in enumerate(TILES):
                            for m in range(2):
                                if i == 0:
                                    pe.wait_ge(s[f"fill{m}"], e * 16 + 16)
                                w = ring[:, m, :].rearrange("p (k f) -> p k f", k=KD)
                                for k in range(KD):
                                    mm = pe.matmul(ps[0:tn, m, :], xT[:, k, t0:t0 + tn], w[:, k, :], start=(k == 0), stop=(k == KD - 1))
                            mm.then_inc(s["hidden"], 1)
                            pe.wait_ge(s["h"], e * 3 + (i + 1))
                            for k in range(KF):
                                mm = pe.transpose(ps[:, 5, k * P:(k + 1) * P], h[:, k * P:(k + 1) * P], ident)
                            mm.then_inc(s["turned"], 1)
                            pe.wait_ge(s["hT"], e * 3 + (i + 1))
                            if i == 0:
                                pe.wait_ge(s["fill2"], e * 16 + 16)
                            w = ring[:, 2, :].rearrange("p (k f) -> p k f", k=KF)
                            for k in range(KF):
                                for hh in range(2):
                                    mm = pe.matmul(ps[0:tn, 2 + hh, :], hT[:, k, 0:tn], w[:, k, HALF * hh:HALF * hh + HALF],
                                                   start=(k == 0), stop=(k == KF - 1))
                            mm.then_inc(s["down"], 1)
                            pe.wait_ge(s["added"], e * 3 + (i + 1))
                        pe.sem_inc(s["used"], 1)

            pe.wait_ge(x_in, 16 * 7)
            band = lambda at, n, g: bands[:, at + g * n:at + (g + 1) * n]
            for c in range(KD):
                g, cols = c // 2, slice(c * P, (c + 1) * P)
                o = ps[:, c, :]
                pe.matmul(o[:, 0:144], x[:, 0, cols], band(B_0, 144, g), start=True, stop=False, skip_group_check=True)
                pe.matmul(o[:, 128:272], x[:, 1, cols], band(B_1, 144, g), start=False, stop=False, skip_group_check=True)
                pe.matmul(o[:, 272:280], pstate[0:120, cols], band(B_S, 8, g)[0:120, :], start=False, stop=False,
                          skip_group_check=True)
                pe.matmul(o[:, 256:280], x[0:24, 2, cols], band(B_2, 24, g)[0:24, :], start=False, stop=True,
                          skip_group_check=True).then_inc(diff_done, 1)
            pe.wait_ge(diff_a, 4)
            pe.wait_ge(diff_d, 4)
            for i, (t0, tn) in enumerate(TILES):
                for g in range(NPG):
                    for k in range(2):
                        mm = pe.matmul(ps[0:tn, 2 * i + g // 2, (g % 2) * PGD:(g % 2 + 1) * PGD], xT[:, 2 * g + k, t0:t0 + tn],
                                       wp[:, g, k, :], start=(k == 0), stop=(k == 1))
                mm.then_inc(pooled, 1)
            pe.wait_ge(prep_in, 16 * 15)
            turn(0, 0)
            turn(0, 1)
            logits(0, 0)
            turn(0, 2)
            logits(0, 1)
            logits(0, 2)
            for k in range(KD):
                mm = pe.transpose(ps[:, 7, k * R_N:(k + 1) * R_N], crow[:, k * P:(k + 1) * P], ident[0:R_N, 0:R_N])
            mm.then_inc(chan_turned, 1)
            pe.wait_ge(state_mul, 2)
            for k in range(KD):
                for hh in range(2):
                    at = KD * R_N + k * NSAMP + 4 * hh
                    mm = pe.matmul(ps[:, 7, at:at + 4], cs_raw[0:120, hh, k * P:(k + 1) * P],
                                   cst[0:120, C_SELB:C_SELB + 4], start=True, stop=True)
            mm.then_inc(vstate_done, 1)
            place(0)
            experts(0)
            overflow(0)
            for i in range(3):
                turn(1, i)
            have_xT(1, 2)
            for e in range(KD):
                n = MIX_BASE + e // 2
                if e % 2 == 0:
                    pe.wait_ge(filled[ring_slot(n)], fills(n))
                w = ring[:, ring_slot(n), :].rearrange("p (k h n) -> p k h n", k=KD, h=2)
                if e >= 4:
                    pe.wait_ge(u_ready, e - 3)
                for hh in range(2):
                    for k in range(KD):
                        mm = pe.matmul(ps[:, 2 * (e % 4) + hh, 0:T], w[:, k, hh, (e % 2) * P:(e % 2 + 1) * P], xT[:, k, :],
                                       start=(k == 0), stop=(k == KD - 1))
                mm.then_inc(ring_free if e % 2 else glu_done, 1)
            pe.wait_ge(u_ready, KD)
            for j in range(TAPS):
                pe.wait_ge(diag_ready, j + 1)
                n = NPROMPT if j < TAPS - 1 else T
                pe.matmul(ps[:, 0, 0:n], diag[:, j % NDIAG, :], u[:, KD - 1, j:j + n], start=(j == 0), stop=(j == TAPS - 1),
                          skip_group_check=True).then_inc(diag_used if j < TAPS - 1 else conv7_done, 1)
            for k in range(KD):
                mm = pe.transpose(ps[0:38, 6 + k // 4, (k % 4) * P:(k % 4 + 1) * P], u[:, k, UW - 38:UW], ident)
                if k % 4 == 3:
                    mm.then_inc(urow_turned, 1)

            def pw_bias(i):
                tn = TILES[i][1]
                for hh in range(2):
                    at = 32 * hh if i == 2 else 0
                    pe.matmul(ps[at:at + tn, 2 * i + hh, :], ones[0:1, 0:tn], bpw[:, HALF * hh:HALF * hh + HALF],
                              start=True, stop=False)

            pw_bias(1)
            pw_bias(2)
            for k in range(KD):
                if k < KD - 1:
                    pe.wait_ge(conv_step, (k + 1) * TAPS if k % 2 == 0 else (k + 2) * TAPS - 1)
                else:
                    pe.wait_ge(conv_done, 1)
                mm = pe.matmul(ps[:, 1, 0:T], mean_w, v[:, k, :], start=(k == 0), stop=(k == KD - 1))
            mm.then_inc(mean_done, 1)
            pe.wait_ge(cent_ready, 2)
            pw_bias(0)
            pe.wait_ge(urow_ready, 2)
            for k in range(KD):
                pe.wait_ge(sq_ready, k + 1)
                mm = pe.matmul(ps[:, 6, 0:T], mean_w, sq[:, k, :], start=(k == 0), stop=(k == KD - 1))
            mm.then_inc(var_done, 1)

            def pointwise(i):
                t0, tn = TILES[i]
                for k in range(KD):
                    n = MIX_BASE + 4 + k // 4
                    if i == 0:
                        pe.wait_ge(act_ready, k + 1)
                        if k % 4 == 0:
                            pe.wait_ge(filled[ring_slot(n)], fills(n))
                    w = ring[:, ring_slot(n), :].rearrange("p (k n) -> p k n", k=4)
                    for hh in range(2):
                        at = 32 * hh if i == 2 else 0
                        mm = pe.matmul(ps[at:at + tn, 2 * i + hh, :], sq[:, k, t0:t0 + tn], w[:, k % 4, HALF * hh:HALF * hh + HALF],
                                       start=False, stop=(k == KD - 1))
                    if i == 2 and k % 4 == 3:
                        mm.then_inc(ring_free, 1)
                if i < 2:
                    mm.then_inc(pw_done, 1)

            pointwise(0)
            pointwise(1)
            turn(2, 0)
            pointwise(2)
            turn(2, 1)
            logits(1, 0)
            turn(2, 2)
            logits(1, 1)
            logits(1, 2)
            place(1)
            experts(1)
            overflow(1)


_INS = ["x_prompt", "x_sample", "state_pool", "state_conv", "meta", "w_pool", "pool_scale", "w_glu", "b_glu", "w_dw",
        "b_dw", "conv_ln_g", "conv_ln_b", "w_pw", "b_pw", "ln_mix_g", "ln_mix_b", "ln_ffn_g", "ln_ffn_b",
        "w_router_group", "w_router_expert", "w_gate", "w_up", "w_down"]
_OUTS = [(1, SEQ, D), (NSAMP, 1, D), (1, 1, PSTATE, D), (1, NSAMP, PSTATE, D), (1, 1, CSTATE, D), (1, NSAMP, CSTATE, D)]


def kernel(**inputs):
    import concourse.bacc as _bacc
    from concourse.bass_utils import run_bass_kernel_spmd as _run

    nc = _bacc.Bacc("TRN2", target_bir_lowering=False, num_devices=1)
    arrays, args = {}, {}
    cst, bands = constants()
    for name, arr in [(n, inputs[n]) for n in _INS] + [("cst", cst), ("bands", bands)]:
        arr = np.ascontiguousarray(arr)
        arrays[f"in_{name}"] = arr
        args[name] = nc.dram_tensor(f"in_{name}", arr.shape, mybir.dt.from_np(arr.dtype), kind="ExternalInput").ap()
    outs = [nc.dram_tensor(f"out_{i}", s, mybir.dt.float32, kind="ExternalOutput").ap() for i, s in enumerate(_OUTS)]
    build(nc, args, outs)
    r = _run(nc, [arrays], core_ids=[0])
    return tuple(r.results[0][f"out_{i}"] for i in range(len(_OUTS)))
```

```python
import concourse.bass as bass
from concourse import mybir
from concourse.alu_op_type import AluOpType as ALU
from contextlib import ExitStack
import numpy as np

D = 1024
F = D // 2
P = 128
KD, KF = D // P, F // P
HALF = 512
META, SEQ, NSAMP = 16, 256, 8
NPROMPT = META + SEQ
T = NPROMPT + NSAMP
TILES = [(0, 128), (128, 128), (256, 24)]
WINDOWS = (2, 4, 8, 16)
NPG, PGD = len(WINDOWS), D // len(WINDOWS)
PSTATE, CSTATE, TAPS = 15, 30, 31
NG, EPG = 4, 8
NE = NG * EPG
QUAD = 4
CAP = P // QUAD
NQ = NE // QUAD
DEPTH = 2
ALPHA = (2.0 * DEPTH) ** 0.25
EPS = 1e-5
CHUNK = 4096
RING = 9
QCHUNKS = 12
TURN = 3
LOOPS = NQ // TURN
REST = range(TURN * LOOPS, NQ)
TURN_FILLS = 32 * TURN * QCHUNKS // RING
MIX_CHUNKS = 6
BASE = [0, NQ * QCHUNKS + MIX_CHUNKS]
MIX_BASE = NQ * QCHUNKS
BIG = 64.0
WARM_BEFORE, WARM_AFTER = 16, 6
SHARED, SHARED_TAPS = 6, 10
GLU_EVERY = 17
GROUPS = [(0, 128), (128, 152)]


def conv_order():
    left = {e: list(range(TAPS if e < SHARED else SHARED_TAPS)) for e in range(SHARED + 1)}
    order, units, since = [(0, None)], 1, 4
    while units < KD or any(left.values()):
        live = [e for e in left if left[e] and e < units][:2]
        if units < KD and (since >= GLU_EVERY or not live):
            order.append((units, None))
            units, since = units + 1, 0
            continue
        for e in live:
            order.append((e, left[e].pop(0)))
            since += 1
    return order


CONV_ORDER = conv_order()
CONV_TAPS = [s for s in CONV_ORDER if s[1] is not None]
DIAG_TAPS = [(e, j) for e in (SHARED, KD - 1) for j in range(SHARED_TAPS if e == SHARED else 0, TAPS)]

C_ID, C_UP, C_ONE, C_IOTA, C_SELB, C_MEAN, C_TIE, C_EPS, C_NTH = 0, 128, 256, 384, 416, 420, 548, 556, 557
C_END = 558
B_0, B_1, B_2, B_S, B_END = 0, 4 * 144, 8 * 144, 8 * 144 + 4 * 24, 8 * 144 + 4 * 24 + 4 * 8
R_BDW, R_G, R_B, R_BA, R_BG, R_N = 31, 32, 33, 34, 35, 36


def constants():
    c = np.zeros((P, C_END), np.float32)
    c[:, C_ID:C_ID + P] = np.eye(P)
    c[:, C_UP:C_UP + P] = np.triu(np.ones((P, P)), 1)
    c[:, C_ONE:C_ONE + P] = 1
    c[:, C_IOTA:C_IOTA + CAP] = np.arange(1, CAP + 1)
    for b in range(4):
        c[b * CSTATE:(b + 1) * CSTATE, C_SELB + b] = 1
    c[:, C_MEAN:C_MEAN + P] = 1.0 / D
    c[:, C_TIE:C_TIE + EPG] = np.arange(EPG) - BIG
    c[:, C_EPS] = EPS
    c[:, C_NTH] = np.arange(1, P + 1)
    bands = np.zeros((P, B_END), np.float32)
    for g, w in enumerate(WINDOWS):
        for p in range(P):
            for j in range(144):
                for at, off in ((B_0, 0), (B_1, P)):
                    if 0 <= j - p < w:
                        bands[p, at + g * 144 + j] = 1.0 / min(off + j + 1, w)
                    if j == p:
                        bands[p, at + g * 144 + j] -= 1
        for p in range(META):
            for j in range(p, min(p + w, META)):
                bands[p, B_2 + g * 24 + j] = 1.0 / w
            bands[p, B_2 + g * 24 + p] -= 1
        for b in range(NSAMP):
            bands[META + b, B_2 + g * 24 + META + b] = 1.0 / w - 1
            for r in range(PSTATE + 1 - w, PSTATE):
                bands[b * PSTATE + r, B_S + g * 8 + b] = 1.0 / w
    return c, bands


def build(nc, a, outs):
    fp32, i32 = mybir.dt.float32, mybir.dt.int32
    ACT = mybir.ActivationFunctionType
    AX = mybir.AxisListType
    y_prompt, y_sample, pool_p, pool_s, conv_p, conv_s = outs

    ctx = ExitStack()
    with ctx:
        def sb(name, shape, dt=fp32):
            return ctx.enter_context(nc.sbuf_tensor(name, shape, dt))

        def sem(name):
            return ctx.enter_context(nc.semaphore(name))

        ring = sb("ring", [P, RING, CHUNK])
        cst = sb("cst", [P, C_END])
        x = sb("x", [P, 3, D])
        z = sb("z", [P, 3, D])
        xT = sb("xT", [P, KD, T])
        gb = sb("gb", [P, 2, D])
        wr = sb("wr", [P, DEPTH, KD, 36])
        lg = sb("lg", [P, 3, 36])
        st = sb("st", [P, 3, 12])
        mv = sb("mv", [P, 3, 2])
        part = sb("part", [P, 3])
        rs = sb("rs", [P, 3])
        warm = sb("warm", [1, 24])
        sm = sb("sm", [P, 16, 3, 8])
        assign = sb("assign", [P, 3, NE])
        gates = sb("gates", [P, 3, NE])
        slot1 = sb("slot1", [P, 3, NE])
        over = sb("over", [P, 3, NE])
        le4 = sb("le4", [P, 3, EPG, NG])
        full = sb("full", [NE, 2])
        full_at = sb("full_at", [NE, NE])
        full_list = sb("full_list", [1, 2, NE], i32)
        cntf = sb("cntf", [1, 1])
        most = sb("most", [1, 1], i32)
        chan = sb("chan", [P, KD, R_N])
        vstate = sb("vstate", [P, KD, NSAMP])
        bpw = x[32:33, 2, :]
        urow = x[64:64 + CSTATE + NSAMP, 2, :]
        U = sb("U", [P, 3104])

        def view(at, n, **k):
            v = U[:, at:at + n]
            return v.rearrange(k.pop("r"), **k) if k else v

        wp = view(0, 2048, r="p (g k n) -> p g k n", g=NPG, k=2)
        prep = ring[:, RING - 1, :]
        cs_raw = prep[:, 0:2 * D].rearrange("p (h n) -> p h n", h=2)
        wrep = prep[:, 2 * D:3 * D]
        zflat = z[:, :, :].rearrange("p i n -> p (i n)")
        bands = zflat[:, 0:B_END]
        pstate = zflat[:, B_END:B_END + D]
        crow = prep[0:R_N, 3 * D:4 * D]
        pscale = xT[:, :, :].rearrange("p a b -> p (a b)")[:, 0:D]
        onehot = view(0, 384, r="p (i s) -> p i s", i=3)
        gated = view(384, 384, r="p (i s) -> p i s", i=3)
        gT = view(768, T)
        xg = view(1056, 1024, r="p (k s) -> p k s", k=KD)
        sil = view(2080, F)
        h = view(2592, F)
        hT = view(2080, F, r="p (k s) -> p k s", k=KF)
        ye = view(1056, D)
        squares = ye
        UW = CSTATE + T
        u = view(0, KD * UW, r="p (k n) -> p k n", k=KD)
        v = zflat[:, 0:KD * T].rearrange("p (k n) -> p k n", k=KD)
        sq = xT
        sg = view(KD * UW, 2 * T, r="p (k n) -> p k n", k=2)
        NDIAG = 6
        diag = zflat[:, KD * T:KD * T + NDIAG * P].rearrange("p (n c) -> p n c", n=NDIAG)
        rstd = view(KD * UW, T)

        ps = ctx.enter_context(nc.psum_tensor("ps", [P, 8, HALF], fp32))

        ident = cst[:, C_ID:C_ID + P]
        upper = cst[:, C_UP:C_UP + P]
        ones = cst[:, C_ONE:C_ONE + P]
        iota1 = cst[:, C_IOTA:C_IOTA + CAP]
        mean_w = cst[:, C_MEAN:C_MEAN + P]
        tie = cst[:, C_TIE:C_TIE + EPG]
        eps = cst[:, C_EPS:C_EPS + 1]

        filled = [sem(f"filled{s}") for s in range(RING)]
        ring_free = sem("ring_free")
        x_in, w_in, prep_in, gb_in, wr_in = (sem(n) for n in ("x_in", "w_in", "prep_in", "gb_in", "wr_in"))
        gb_spread, gb_copied = sem("gb_spread"), sem("gb_copied")
        outs_done = sem("outs_done")
        zeroed = sem("zeroed")
        wp_scaled = sem("wp_scaled")
        state_mul = sem("state_mul")
        diff_done, diff_a, diff_d, pooled = (sem(n) for n in ("diff_done", "diff_a", "diff_d", "pooled"))
        chan_turned, vstate_done = sem("chan_turned"), sem("vstate_done")
        prep_done = sem("prep_done")
        chain = sem("chain")
        root_in, root_out, normed, crt_out = (
            sem(n) for n in ("root_in", "root_out", "normed", "crt_out"))
        moment_step = sem("moment_step")
        turned, xT_ready = sem("turned"), sem("xT_ready")
        diag_ready, diag_used, diag_summed = sem("diag_ready"), sem("diag_used"), sem("diag_summed")
        logits_done, exp_in, exp_out, routed, placed, most_ready = (
            sem(n) for n in ("logits_done", "exp_in", "exp_out", "routed", "placed", "most_ready"))
        residual = sem("residual")
        onehot_ready, gated_ready, dispatched, gT_turned, gT_ready, xg_a, xg_d = (
            sem(n) for n in ("onehot_ready", "gated_ready", "dispatched", "gT_turned", "gT_ready", "xg_a", "xg_d"))
        silu_done, h_ready, hT_turned, hT_ready, ye_a, ye_d, combined, added = (
            sem(n) for n in ("silu_done", "h_ready", "hT_turned", "hT_ready", "ye_a", "ye_d", "combined", "added"))
        glu_done, sig_ready, u_ready, conv_step, conv_done = (
            sem(n) for n in ("glu_done", "sig_ready", "u_ready", "conv_step", "conv_done"))
        mean_done, cent_ready, sq_ready, var_done, vn_ready, act_ready, pw_done, urow_turned, urow_ready = (
            sem(n) for n in ("mean_done", "cent_ready", "sq_ready", "var_done", "vn_ready", "act_ready",
                             "pw_done", "urow_turned", "urow_ready"))
        fb = []
        for L in range(DEPTH):
            fb.append({n: sem(f"over{L}_{n}") for n in (
                "fill0", "fill1", "fill2", "used", "hidden", "silu", "h", "turned", "hT", "down", "added",
                "gates", "counts", "listed")})

        block = ctx.enter_context(nc.Block())

        ORDER = ((0, 1, 2), (0, 1, 2), (0, 2, 1), (0, 1, 2))

        def nth(n, i):
            return 3 * n + ORDER[n].index(i) + 1

        def turns(m, i):
            return 5 * m + sum(2 if j < 2 else 1 for j in ORDER[m][:ORDER[m].index(i)])

        ROOTS = (0, 3, 4, 7)
        ROOT_D = 32
        assert ROOT_D * ROOT_D == D
        COMBINE = ((0, 0, 4, 0), (1, 0, 5, 0), (2, 0, 6, 0), (0, 1, 7, 0), (1, 1, 2, 0), (2, 1, 6, 32))

        def ring_slot(n):
            return n % RING

        def turn_bank(m, i):
            return ((0, 2, 4) if m != 1 else (4, 6, 4))[i]

        def fills(n):
            return 32 * (n // RING + 1)

        def listed(eng, r):
            return eng.value_load(full_list[0:1, 0, bass.ds(eng.snap(r), 1)], min_val=0, max_val=NE)

        def listed_index(eng, r):
            return eng.value_load(full_list[0:1, 1, bass.ds(eng.snap(r), 1)], min_val=0, max_val=NE - 1)

        def used_up(n):
            return RING + n + 1

        @block.sync
        def _(sp):
            mt, xp, xs = a["meta"], a["x_prompt"], a["x_sample"]
            sp.dma_start(x[0:META, 0, :], mt).then_inc(x_in, 16)
            sp.dma_start(x[META:P, 0, :], xp[0, 0:112, :]).then_inc(x_in, 16)
            sp.dma_start(x[:, 1, :], xp[0, 112:240, :]).then_inc(x_in, 16)
            sp.dma_start(x[0:16, 2, :], xp[0, 240:256, :]).then_inc(x_in, 16)
            sp.dma_start(x[16:24, 2, :], xs[:, 0, :]).then_inc(x_in, 16)
            sp.dma_start(pstate[0:120, :], a["state_pool"][0].rearrange("b j d -> (b j) d")).then_inc(x_in, 16)
            sp.dma_start(bands, a["bands"]).then_inc(x_in, 16)
            sp.dma_start(wp, a["w_pool"][0].rearrange("g (k p) n -> p g k n", p=P)).then_inc(w_in, 16)
            sp.dma_start(pscale, a["pool_scale"][0:1, :].broadcast_to([P, D])).then_inc(w_in, 16)
            sp.dma_start(cst[:, :], a["cst"]).then_inc(w_in, 16)
            sp.dma_start(gb[:, 0, :], a["ln_mix_g"][0:1, :].broadcast_to([P, D])).then_inc(gb_in, 16)
            sp.dma_start(gb[:, 1, :], a["ln_mix_b"][0:1, :].broadcast_to([P, D])).then_inc(gb_in, 16)
            sp.dma_start(crow[0:TAPS, :], a["w_dw"][0]).then_inc(prep_in, 16)
            sp.dma_start(crow[R_BDW:R_BDW + 1, :], a["b_dw"]).then_inc(prep_in, 16)
            sp.dma_start(crow[R_G:R_G + 1, :], a["conv_ln_g"]).then_inc(prep_in, 16)
            sp.dma_start(crow[R_B:R_B + 1, :], a["conv_ln_b"]).then_inc(prep_in, 16)
            sp.dma_start(crow[R_BA:R_BG + 1, :], a["b_glu"].rearrange("o (h n) -> (o h) n", h=2)).then_inc(prep_in, 16)
            sp.dma_start(cs_raw[0:120, :, :], a["state_conv"][0].rearrange("(h b) j d -> (b j) h d", h=2)).then_inc(prep_in, 16)
            for b in range(4):
                sp.dma_start(wrep[b * CSTATE:(b + 1) * CSTATE, :], a["w_dw"][0, 0:CSTATE, :]).then_inc(prep_in, 16)
            sp.sem_inc(ring_free, RING)

            def load(n, parts, count=None):
                sp.wait_ge(ring_free, n + 1 if count is None else count)
                if n == RING - 1:
                    sp.wait_ge(prep_done, 1)
                for dst, src in parts:
                    sp.dma_start(dst, src).then_inc(filled[ring_slot(n)], 32 // len(parts))

            def experts(L):
                up = [a[w][L].rearrange("e (k p) f -> p e k f", p=P) for w in ("w_gate", "w_up")]
                down = a["w_down"][L].rearrange("e (k p) n -> p e k n", p=P)
                def quad(it, b):
                    first = sp.snap(it * (TURN * QUAD) + QUAD * b) if b < TURN else QUAD * b
                    for c in range(QCHUNKS):
                        n = BASE[L] + QCHUNKS * b + c
                        dst = ring[:, ring_slot(n), :].rearrange("p (e k f) -> p e k f", e=QUAD, k=2)
                        if c < 8:
                            parts = [(dst[:, :, k, :], up[c // 4][:, bass.ds(first, QUAD), 2 * (c % 4) + k, :])
                                     for k in range(2)]
                        else:
                            half, k0 = (c - 8) // 2, 2 * (c % 2)
                            parts = [(dst[:, :, k, :], down[:, bass.ds(first, QUAD), k0 + k, HALF * half:HALF * half + HALF])
                                     for k in range(2)]
                        load(n, parts, it * (TURN * QCHUNKS) + (n + 1))

                with sp.Fori(0, LOOPS) as it:
                    for b in range(TURN):
                        quad(it, b)
                for b in REST:
                    quad(0, b)

            def overflow(L):
                s = fb[L]
                sp.wait_ge(most_ready, L + 1)
                count = sp.value_load(most[0:1, 0:1], min_val=0, max_val=T)
                with sp.If(count > CAP):
                    sp.wait_ge(ring_free, RING + BASE[L] + NQ * QCHUNKS)
                    sp.wait_ge(s["listed"], 5)
                    with sp.Fori(0, NE) as r:
                        with sp.If(listed(sp, r) > 0):
                            ee = listed_index(sp, r)
                            for m, w in enumerate(("w_gate", "w_up", "w_down")):
                                kk = 4 if m == 2 else 8
                                src = a[w][L][bass.ds(ee, 1), :, :].rearrange("o (k p) f -> p (o k) f", p=P)
                                dst = ring[:, m, :].rearrange("p (k f) -> p k f", k=kk)
                                sp.wait_ge(s["used"], r + 1)
                                sp.dma_start(dst, src).then_inc(s[f"fill{m}"], 16)
                    sp.wait_ge(s["used"], NE + 1)

            experts(0)
            overflow(0)
            glu = a["w_glu"][0].rearrange("(k p) (h n) -> p k h n", p=P, h=2)
            for j in range(4):
                n = MIX_BASE + j
                dst = ring[:, ring_slot(n), :].rearrange("p (k h n) -> p k h n", k=KD, h=2)
                load(n, [(dst[:, :, hh, :], glu[:, :, hh, 256 * j:256 * j + 256]) for hh in range(2)])
            for j in range(2):
                n = MIX_BASE + 4 + j
                load(n, [(ring[:, ring_slot(n), :].rearrange("p (k n) -> p k n", k=4),
                          a["w_pw"][0, 512 * j:512 * j + 512, :].rearrange("(k p) n -> p k n", p=P))])
            experts(1)
            overflow(1)
            sp.wait_ge(normed, 10)
            sp.dma_start(y_prompt[0, 0:112, :], x[META:P, 0, :]).then_inc(outs_done, 16)
            sp.wait_ge(normed, 11)
            sp.dma_start(y_prompt[0, 112:240, :], x[:, 1, :]).then_inc(outs_done, 16)
            sp.wait_ge(normed, 12)
            sp.dma_start(y_prompt[0, 240:256, :], x[0:16, 2, :]).then_inc(outs_done, 16)
            sp.dma_start(y_sample[:, 0, :], x[16:24, 2, :]).then_inc(outs_done, 16)
            sp.wait_ge(outs_done, 16 * 10)

        @block.gpsimd
        def _(pool):
            for t in (lg, assign, gates, slot1, over, sm):
                pool.memset(t[:], 0.0).then_inc(zeroed, 1)
            pool.memset(warm[:], 1.0).then_inc(zeroed, 1)
            pool.wait_ge(prep_in, 16 * 11)
            for hh in range(2):
                pool.tensor_tensor(out=cs_raw[0:120, hh, :], in0=cs_raw[0:120, hh, :], in1=wrep[0:120, :],
                                   op=ALU.mult).then_inc(state_mul, 1)

        @block.scalar
        def _(act):
            def load_router(L):
                act.dma_start(wr[:, L, :, 0:NG], a["w_router_group"][L].rearrange("(k p) n -> p k n", p=P)).then_inc(wr_in, 16)
                act.dma_start(wr[:, L, :, NG:NG + NE], a["w_router_expert"][L].rearrange("(k p) n -> p k n", p=P)).then_inc(wr_in, 16)

            act.wait_ge(x_in, 16 * 7)
            load_router(0)
            act.dma_start(bpw, a["b_pw"]).then_inc(prep_in, 16)

            def load_gb(n):
                g, b = (("ln_mix_g", "ln_mix_b"), ("ln_ffn_g", "ln_ffn_b"))[n % 2]
                L = n // 2
                act.wait_ge(normed, 3 * n)
                for k, w in enumerate((g, b)):
                    if n % 2:
                        act.dma_start(gb[0:1, k, :], a[w][L:L + 1, :]).then_inc(gb_in, 16)
                    else:
                        act.dma_start(gb[:, k, :], a[w][L:L + 1, :].broadcast_to([P, D])).then_inc(gb_in, 16)

            preloads = [0]

            def preload(func):
                preloads[0] += 1
                act.activation(warm[:, preloads[0]:preloads[0] + 1], warm[:, 0:1], func)

            def root(n, i):
                tn = TILES[i][1]
                act.wait_ge(root_in, ROOTS[n] + ORDER[n].index(i) + 1)
                act.activation(mv[0:tn, i, 1:2], mv[0:tn, i, 1:2], ACT.Sqrt, bias=eps[0:tn, :]).then_inc(root_out, 1)

            moment_steps = [0]

            def step(ins):
                moment_steps[0] += 1
                ins.then_inc(moment_step, 1)
                act.wait_ge(moment_step, moment_steps[0])

            def moments(n):
                act.wait_ge(added, 6 * NQ * (n // 2 + 1))
                for i in (1, 2):
                    tn = TILES[i][1]
                    step(act.activation(squares[0:tn, :], z[0:tn, i, :], ACT.Copy, scale=-1.0 / (D * ROOT_D),
                                        accum_out=part[0:tn, i:i + 1]))
                    step(act.activation(squares[0:tn, :], z[0:tn, i, :], ACT.Square, scale=1.0 / ROOT_D, bias=part[0:tn, i:i + 1],
                                        accum_out=mv[0:tn, i, 1:2]))
                    if i == 1:
                        root(n, 0)
                    step(act.activation(mv[0:tn, i, 0:1], part[0:tn, i:i + 1], ACT.Copy, scale=float(ROOT_D)))
                    act.activation(mv[0:tn, i, 1:2], mv[0:tn, i, 1:2], ACT.Sqrt, bias=eps[0:tn, :]).then_inc(root_out, 1)

            def turn(m, i):
                t0, tn = TILES[i]
                for k in range(2 if i < 2 else 1):
                    act.wait_ge(turned, turns(m, i) + k + 1)
                    if i < 2:
                        act.activation(xT[:, 4 * k:4 * k + 4, t0:t0 + tn], ps[:, turn_bank(m, i) + k, :].rearrange("p (k t) -> p k t", k=4),
                                       ACT.Copy).then_inc(xT_ready, 1)
                    else:
                        act.activation(xT[:, :, t0:t0 + tn], ps[:, turn_bank(m, i), 0:KD * tn].rearrange("p (k t) -> p k t", k=KD),
                                       ACT.Copy).then_inc(xT_ready, 1)

            def norm_route(L):
                n, m = 2 * L, 2 * L
                first, second, third = ORDER[n]
                root(n, first)
                root(n, second)
                turn(m, first)
                turn(m, second)
                root(n, third)
                preload(ACT.Exp)
                if L == 0:
                    load_gb(1)
                turn(m, third)
                for k in range(2):
                    act.wait_ge(exp_in, 2 * L + k + 1)
                    t = sm[:, 0, :, 0:NG] if k == 0 else sm[:, 9, :, 0:1]
                    o = sm[:, 1, :, 0:NG] if k == 0 else sm[:, 10, :, 0:1]
                    act.activation(o, t, ACT.Exp).then_inc(exp_out, 1)
                act.wait_ge(normed, 6 * L + 3)
                for i, (t0, tn) in enumerate(TILES):
                    act.activation(z[0:tn, i, :], x[0:tn, i, :], ACT.Copy, scale=ALPHA).then_inc(residual, 1)
                preload(ACT.Silu)

            def experts(L):
                def quad(it, b):
                    q = NQ * L + b + 1
                    done = it * TURN + q
                    act.wait_ge(dispatched, it * (2 * TURN) + (2 * q - 1))
                    act.activation(xg[:, 0:4, :], ps[:, 6, :].rearrange("p (k s) -> p k s", k=4), ACT.Copy).then_inc(xg_a, 1)
                    through = it * (TURN * QCHUNKS) + used_up(BASE[L] + QCHUNKS * b - 1)
                    if b == NQ - 1:
                        for k in range(4):
                            act.wait_ge(gb_spread, 4 * L + k + 1)
                            act.activation(gb[:, k // 2, HALF * (k % 2):HALF * (k % 2) + HALF], ps[:, 2 + k, :],
                                           ACT.Copy).then_inc(gb_copied, 1)
                    act.wait_ge(ring_free, through + 4)
                    act.activation(sil, ps[:, 0, :], ACT.Silu).then_inc(silu_done, 1)
                    act.wait_ge(hT_turned, done)
                    act.activation(hT, ps[:, 5, :].rearrange("p (k s) -> p k s", k=KF), ACT.Copy).then_inc(hT_ready, 1)
                    act.wait_ge(ring_free, through + 10)
                    act.activation(ye[:, 0:HALF], ps[:, 2, :], ACT.Copy).then_inc(ye_a, 1)

                with act.Fori(0, LOOPS) as it:
                    for b in range(TURN):
                        quad(it, b)
                for b in REST:
                    quad(0, b)

            def overflow(L):
                s = fb[L]
                act.wait_ge(most_ready, L + 1)
                count = act.value_load(most[0:1, 0:1], min_val=0, max_val=T)
                with act.If(count > CAP):
                    act.wait_ge(s["listed"], 5)
                    with act.Fori(0, NE) as r:
                        with act.If(listed(act, r) > 0):
                            for i, (t0, tn) in enumerate(TILES):
                                act.wait_ge(s["hidden"], r * 3 + (i + 1))
                                act.activation(sil[0:tn, :], ps[0:tn, 0, :], ACT.Silu).then_inc(s["silu"], 1)
                                act.wait_ge(s["turned"], r * 3 + (i + 1))
                                act.activation(hT, ps[:, 5, :].rearrange("p (k s) -> p k s", k=KF), ACT.Copy).then_inc(s["hT"], 1)
                    act.wait_ge(s["used"], NE + 1)

            act.wait_ge(zeroed, 7)
            preload(ACT.Sqrt)
            for c in range(0, KD, 2):
                act.wait_ge(diff_done, c + 1)
                if c == 0:
                    act.wait_ge(wp_scaled, 1)
                act.activation(xT[:, c, :], ps[:, c, 0:T], ACT.Copy).then_inc(diff_a, 1)
            norm_route(0)
            experts(0)
            overflow(0)
            preload(ACT.Sqrt)
            moments(1)
            turn(1, 0)
            preload(ACT.Sigmoid)
            turn(1, 1)
            turn(1, 2)
            load_gb(2)
            load_router(1)
            act.dma_start(pool_p[0, 0], a["x_prompt"][0, SEQ - PSTATE:SEQ, :]).then_inc(outs_done, 16)
            act.dma_start(pool_s[0, :, 0:PSTATE - 1, :], a["state_pool"][0, :, 1:PSTATE, :]).then_inc(outs_done, 16)
            act.dma_start(pool_s[0, :, PSTATE - 1, :], a["x_sample"][:, 0, :]).then_inc(outs_done, 16)
            act.dma_start(conv_s[0, :, 0:CSTATE - 1, :], a["state_conv"][0, :, 1:CSTATE, :]).then_inc(outs_done, 16)
            for e in range(KD):
                if e % 2:
                    act.wait_ge(ring_free, used_up(MIX_BASE + e // 2))
                else:
                    act.wait_ge(glu_done, e // 2 + 1)
                if e >= 2:
                    act.wait_ge(u_ready, e - 1)
                act.activation(sg[:, e % 2, :], ps[:, 2 * (e % 4) + 1, 0:T], ACT.Sigmoid,
                               bias=chan[:, e, R_BG:R_BG + 1]).then_inc(sig_ready, 1)
            for n, (e, j) in enumerate(DIAG_TAPS):
                if n >= NDIAG:
                    act.wait_ge(diag_used, n - NDIAG + 1)
                act.activation(diag[:, n % NDIAG, :], ident, ACT.Copy, scale=chan[:, e, j:j + 1]).then_inc(diag_ready, 1)
            for k in range(2):
                act.wait_ge(urow_turned, k + 1)
                act.activation(urow[0:38, HALF * k:HALF * k + HALF], ps[64 * k:64 * k + 38, 4, :], ACT.Copy).then_inc(urow_ready, 1)
            act.wait_ge(urow_ready, 2)
            act.dma_start(conv_p[0, 0], urow[0:CSTATE, :]).then_inc(outs_done, 16)
            act.dma_start(conv_s[0, :, CSTATE - 1, :], urow[CSTATE:CSTATE + NSAMP, :]).then_inc(outs_done, 16)
            preload(ACT.Sqrt)
            for g, (t0, tn) in enumerate(GROUPS):
                for k in range(2):
                    act.wait_ge(cent_ready, 2 * g + k + 1)
                    act.activation(sq[:, 4 * k:4 * k + 4, t0:t0 + tn], v[:, 4 * k:4 * k + 4, t0:t0 + tn], ACT.Square).then_inc(sq_ready, 1)
            for g, (t0, tn) in enumerate(GROUPS):
                if g:
                    preload(ACT.Sqrt)
                act.wait_ge(var_done, g + 1)
                act.activation(rstd[:, t0:t0 + tn], ps[:, 7 - 2 * g, 0:tn], ACT.Sqrt, bias=eps).then_inc(crt_out, 1)
                preload(ACT.Silu)
                for e in range(KD):
                    act.wait_ge(vn_ready, 2 * g + e // 4 + 1)
                    act.activation(sq[:, e, t0:t0 + tn], v[:, e, t0:t0 + tn], ACT.Silu, bias=chan[:, e, R_B:R_B + 1],
                                   scale=chan[:, e, R_G:R_G + 1]).then_inc(act_ready, 1)
            preload(ACT.Sqrt)
            norm_route(1)
            load_gb(3)
            experts(1)
            overflow(1)
            preload(ACT.Sqrt)
            moments(3)

        @block.vector
        def _(dve):
            steps = [0]

            def link(ins):
                steps[0] += 1
                ins.then_inc(chain, 1)
                dve.wait_ge(chain, steps[0])

            def stats(i):
                tn = TILES[i][1]
                for k in range(2):
                    ins = dve.bn_stats(st[0:tn, i, 6 * k:6 * k + 6], z[0:tn, i, HALF * k:HALF * k + HALF])
                link(ins)
                dve.bn_aggr(mv[0:tn, i, :], st[0:tn, i, :]).then_inc(root_in, 1)

            def normalise(n, i):
                tn = TILES[i][1]
                if i == 0 and n % 2:
                    dve.wait_ge(gb_copied, 4 * (n // 2 + 1))
                elif i == 0:
                    dve.wait_ge(gb_in, 32 * (n + 1))
                by_act = n % 2 == 1 and i > 0
                if by_act:
                    dve.wait_ge(root_out, nth(n, i))
                else:
                    dve.wait_ge(root_in, ROOTS[n] + ORDER[n].index(i) + 1)
                dve.scalar_tensor_tensor(out=z[0:tn, i, :], in0=z[0:tn, i, :], scalar=mv[0:tn, i, 0:1], in1=gb[0:tn, 0, :],
                                         op0=ALU.add if by_act else ALU.subtract, op1=ALU.mult)
                dve.wait_ge(root_out, nth(n, i))
                link(dve.reciprocal(rs[0:tn, i:i + 1], mv[0:tn, i, 1:2]))
                dve.scalar_tensor_tensor(out=x[0:tn, i, :], in0=z[0:tn, i, :], scalar=rs[0:tn, i:i + 1], in1=gb[0:tn, 1, :],
                                         op0=ALU.mult, op1=ALU.add).then_inc(normed, 1)

            def layer_norm(n):
                for i in ORDER[n]:
                    if n == 2:
                        residual_pw(i)
                    else:
                        if n == 0:
                            residual_pool(i)
                        if n == 0 or i == 0:
                            stats(i)
                    normalise(n, i)

            def residual_pool(i):
                t0, tn = TILES[i]
                dve.wait_ge(pooled, i + 1)
                link(dve.scalar_tensor_tensor(out=z[0:tn, i, :].rearrange("p (h n) -> p h n", h=2),
                                              in0=x[0:tn, i, :].rearrange("p (h n) -> p h n", h=2), scalar=ALPHA,
                                              in1=ps[0:tn, 2 * i:2 * i + 2, :], op0=ALU.mult, op1=ALU.add))

            def residual_pw(i):
                tn = TILES[i][1]
                if i == 0:
                    dve.wait_ge(act_ready, 2 * KD)
                for hh in range(2):
                    if i == 1 and hh:
                        dve.wait_ge(ring_free, used_up(MIX_BASE + MIX_CHUNKS - 1))
                    else:
                        dve.wait_ge(pw_done, (1 + hh, 4, 3)[i])
                    cols = slice(HALF * hh, HALF * hh + HALF)
                    at, bank = (32 * hh, 4) if i == 2 else (0, 2 * i + hh)
                    link(dve.scalar_tensor_tensor(out=z[0:tn, i, cols], in0=x[0:tn, i, cols], scalar=ALPHA,
                                                  in1=ps[at:at + tn, bank, :], op0=ALU.mult, op1=ALU.add))
                    if i == 2:
                        link(dve.tensor_tensor(out=z[0:tn, i, cols], in0=z[0:tn, i, cols],
                                               in1=ps[64 + at:64 + at + tn, bank, :], op=ALU.add))
                    ins = dve.bn_stats(st[0:tn, i, 6 * hh:6 * hh + 6], z[0:tn, i, cols])
                link(ins)
                dve.bn_aggr(mv[0:tn, i, :], st[0:tn, i, :]).then_inc(root_in, 1)

            def first_best(val, out):
                n = val.shape[2]
                cand, low = sm[:, 12, :, 0:n], sm[:, 13, :, 0:1]
                link(dve.scalar_tensor_tensor(out=cand, in0=val, scalar=0.0, in1=tie[:, 0:n].unsqueeze(1).broadcast_to([P, 3, n]),
                                              op0=ALU.is_equal, op1=ALU.mult))
                link(dve.tensor_reduce(low, cand, AX.X, ALU.min))
                link(dve.tensor_tensor(out=out, in0=cand, in1=low.broadcast_to([P, 3, n]), op=ALU.is_equal))

            def route(L):
                dve.wait_ge(logits_done, L + 1)
                if L == 0:
                    dve.wait_ge(zeroed, 7)
                link(dve.tensor_copy(lg[:, 0:2, :], ps[:, 6, 0:72].rearrange("p (i n) -> p i n", i=2)))
                link(dve.tensor_copy(lg[0:24, 2, :], ps[0:24, 6, 72:108]))
                grp, gs, eg = lg[:, :, 0:NG], sm[:, 0, :, 0:NG], sm[:, 1, :, 0:NG]
                m, ohg, pg = sm[:, 2, :, 0:1], sm[:, 3, :, 0:NG], sm[:, 4, :, 0:1]
                link(dve.tensor_reduce(m, grp, AX.X, ALU.max))
                dve.tensor_tensor(out=gs, in0=grp, in1=m.broadcast_to([P, 3, NG]), op=ALU.subtract).then_inc(exp_in, 1)
                dve.wait_ge(exp_in, 2 * L + 1)
                first_best(gs, ohg)
                link(dve.tensor_tensor(out=le4[:, :, :, :], in0=lg[:, :, NG:NG + NE].rearrange("p i (g e) -> p i e g", g=NG),
                                       in1=ohg.unsqueeze(2).broadcast_to([P, 3, EPG, NG]), op=ALU.mult))
                le, oh1, oh2, d2 = sm[:, 5, :, :], sm[:, 6, :, :], sm[:, 7, :, :], sm[:, 8, :, :]
                link(dve.tensor_reduce(le, le4[:, :, :, :], AX.X, ALU.add))
                m1, m2, e2 = sm[:, 11, :, 0:1], sm[:, 9, :, 0:1], sm[:, 10, :, 0:1]
                link(dve.tensor_reduce(m1, le, AX.X, ALU.max))
                link(dve.tensor_tensor(out=le, in0=le, in1=m1.broadcast_to([P, 3, EPG]), op=ALU.subtract))
                first_best(le, oh1)
                link(dve.scalar_tensor_tensor(out=d2, in0=oh1, scalar=-3e38, in1=le, op0=ALU.mult, op1=ALU.add))
                dve.tensor_reduce(m2, d2, AX.X, ALU.max).then_inc(exp_in, 1)
                dve.wait_ge(exp_in, 2 * L + 2)
                link(dve.tensor_tensor(out=d2, in0=d2, in1=m2.broadcast_to([P, 3, EPG]), op=ALU.subtract))
                first_best(d2, oh2)
                link(dve.tensor_tensor(out=d2, in0=oh1, in1=oh2, op=ALU.add))

                def spread(out, in8):
                    return dve.tensor_tensor(out=out[:, :, :].rearrange("p i (g e) -> p i g e", g=NG),
                                             in0=ohg.unsqueeze(3).broadcast_to([P, 3, NG, EPG]),
                                             in1=in8.unsqueeze(2).broadcast_to([P, 3, NG, EPG]), op=ALU.mult)
                spread(assign, d2).then_inc(routed, 1)
                dve.wait_ge(routed, L + 1)
                dve.wait_ge(exp_out, 2 * L + 2)
                g1, g2, den = sm[:, 14, :, 0:1], sm[:, 14, :, 1:2], sm[:, 14, :, 2:3]
                link(dve.tensor_reduce(pg, eg, AX.X, ALU.add))
                link(dve.scalar_tensor_tensor(out=den, in0=e2, scalar=1.0, in1=pg, op0=ALU.add, op1=ALU.mult))
                link(dve.reciprocal(g1, den))
                link(dve.tensor_tensor(out=g2, in0=g1, in1=e2, op=ALU.mult))
                link(dve.tensor_tensor(out=oh1, in0=oh1, in1=g1.broadcast_to([P, 3, EPG]), op=ALU.mult))
                link(dve.tensor_tensor(out=oh2, in0=oh2, in1=g2.broadcast_to([P, 3, EPG]), op=ALU.mult))
                link(dve.tensor_tensor(out=oh1, in0=oh1, in1=oh2, op=ALU.add))
                link(spread(gates, oh1))
                dve.wait_ge(placed, L + 1)
                for k, (i0, i1, n) in enumerate(((0, 2, P), (2, 3, 24))):
                    link(dve.scalar_tensor_tensor(
                        out=slot1[0:n, i0:i1, :], in0=ps[0:n, 5, NE * i0:NE * i1].rearrange("p (i e) -> p i e", e=NE),
                        scalar=1.0, in1=assign[0:n, i0:i1, :], op0=ALU.add, op1=ALU.mult))
                link(dve.tensor_reduce(cntf[:, :], ps[0:1, 5, 3 * NE:4 * NE], AX.X, ALU.max))
                dve.tensor_copy(most[:, :], cntf[:, :]).then_inc(most_ready, 1)

            def experts(L):
                dve.wait_ge(residual, 3 * L + 3)
                def quad(it, b):
                    q = NQ * L + b + 1
                    done = it * TURN + q
                    first = dve.snap(it * (TURN * QUAD) + QUAD * b) if b < TURN else QUAD * b
                    rows = lambda t: t[:, :, bass.ds(first, QUAD)].unsqueeze(3).broadcast_to([P, 3, QUAD, CAP])
                    cols = lambda t: t.rearrange("p i (e s) -> p i e s", e=QUAD)
                    dve.tensor_tensor(out=cols(onehot), in0=rows(slot1),
                                      in1=iota1.unsqueeze(1).unsqueeze(1).broadcast_to([P, 3, QUAD, CAP]),
                                      op=ALU.is_equal).then_inc(onehot_ready, 1)
                    dve.wait_ge(onehot_ready, done)
                    dve.tensor_tensor(out=cols(gated), in0=cols(onehot), in1=rows(gates), op=ALU.mult).then_inc(gated_ready, 1)
                    dve.wait_ge(dispatched, it * (2 * TURN) + 2 * q)
                    dve.tensor_copy(xg[:, 4:8, :], ps[:, 7, :].rearrange("p (k s) -> p k s", k=4)).then_inc(xg_d, 1)
                    dve.wait_ge(silu_done, done)
                    through = it * (TURN * QCHUNKS) + used_up(BASE[L] + QCHUNKS * b - 1)
                    dve.wait_ge(ring_free, through + 8)
                    dve.tensor_tensor(out=h, in0=sil, in1=ps[:, 1, :], op=ALU.mult).then_inc(h_ready, 1)
                    dve.wait_ge(gT_turned, done)
                    dve.tensor_copy(gT, ps[:, 4, 0:T]).then_inc(gT_ready, 1)
                    for j, (i, k, bank, at) in enumerate(COMBINE):
                        if j == 3:
                            dve.wait_ge(ring_free, through + 12)
                            dve.tensor_copy(ye[:, HALF:D], ps[:, 3, :]).then_inc(ye_d, 1)
                        n = TILES[i][1]
                        dve.wait_ge(combined, it * (6 * TURN) + (6 * (q - 1) + j + 1))
                        zz = z[0:n, i, HALF * k:HALF * k + HALF]
                        dve.tensor_tensor(out=zz, in0=zz, in1=ps[at:at + n, bank, :], op=ALU.add).then_inc(added, 1)

                with dve.Fori(0, LOOPS) as it:
                    for b in range(TURN):
                        quad(it, b)
                for b in REST:
                    quad(0, b)

            def overflow(L):
                s = fb[L]
                dve.wait_ge(most_ready, L + 1)
                count = dve.value_load(most[0:1, 0:1], min_val=0, max_val=T)
                with dve.If(count > CAP):
                    dve.scalar_tensor_tensor(out=over[:, :, :], in0=slot1[:, :, :], scalar=CAP + 0.5,
                                             in1=gates[:, :, :], op0=ALU.is_gt, op1=ALU.mult).then_inc(s["gates"], 1)
                    dve.wait_ge(s["gates"], 1)
                    dve.wait_ge(s["counts"], 1)
                    dve.tensor_scalar(full[:, 0:1], ps[0:NE, 5, 0:1], CAP + 0.5, None, ALU.is_gt).then_inc(s["listed"], 1)
                    dve.wait_ge(s["counts"], 2)
                    dve.scalar_tensor_tensor(out=full[:, 1:2], in0=ps[0:NE, 5, 1:2], scalar=1.0, in1=full[:, 0:1],
                                             op0=ALU.add, op1=ALU.mult).then_inc(s["listed"], 1)
                    dve.wait_ge(s["listed"], 2)
                    dve.tensor_scalar(full_at[:, :], iota1[0:NE, :], full[:, 1:2], None, ALU.is_equal).then_inc(s["listed"], 1)
                    dve.wait_ge(s["counts"], 3)
                    dve.tensor_copy(full_list[:, 0, :], ps[0:1, 5, 2:2 + NE]).then_inc(s["listed"], 1)
                    dve.tensor_scalar(full_list[:, 1, :], ps[0:1, 5, 2:2 + NE], -1.0, 0.0, ALU.add, ALU.max).then_inc(s["listed"], 1)
                    dve.wait_ge(s["listed"], 5)
                    with dve.Fori(0, NE) as r:
                        with dve.If(listed(dve, r) > 0):
                            ee = listed_index(dve, r)
                            for i, (t0, tn) in enumerate(TILES):
                                dve.wait_ge(s["silu"], r * 3 + (i + 1))
                                dve.tensor_tensor(out=h[0:tn, :], in0=sil[0:tn, :], in1=ps[0:tn, 1, :], op=ALU.mult).then_inc(s["h"], 1)
                                dve.wait_ge(s["down"], r * 3 + (i + 1))
                                zz = z[0:tn, i, :].rearrange("p (h n) -> p h n", h=2)
                                dve.scalar_tensor_tensor(out=zz, in0=ps[0:tn, 2:4, :], scalar=over[0:tn, i, bass.ds(ee, 1)],
                                                         in1=zz, op0=ALU.mult, op1=ALU.add).then_inc(s["added"], 1)
                    dve.wait_ge(s["used"], NE + 1)
                dve.wait_ge(added, 6 * NQ * (L + 1))

            dve.wait_ge(w_in, 48)
            dve.tensor_tensor(out=wp, in0=wp, in1=pscale.rearrange("p (g n) -> p g n", g=NPG).unsqueeze(2)
                              .broadcast_to([P, NPG, 2, PGD]), op=ALU.mult).then_inc(wp_scaled, 1)
            for c in range(1, KD, 2):
                dve.wait_ge(diff_done, c + 1)
                if c == 1:
                    dve.wait_ge(wp_scaled, 1)
                dve.tensor_copy(xT[:, c, :], ps[:, c, 0:T]).then_inc(diff_d, 1)
            layer_norm(0)
            route(0)
            dve.wait_ge(chan_turned, 1)
            link(dve.tensor_copy(chan[:, :, :], ps[:, 7, 0:KD * R_N].rearrange("p (k r) -> p k r", k=KD)))
            dve.wait_ge(vstate_done, 2)
            dve.tensor_tensor(out=vstate[:, :, :], in0=ps[:, 7, KD * R_N:KD * R_N + KD * NSAMP].rearrange("p (k b) -> p k b", k=KD),
                              in1=chan[:, :, R_BDW:R_BDW + 1].broadcast_to([P, KD, NSAMP]), op=ALU.add).then_inc(prep_done, 1)
            experts(0)
            overflow(0)
            layer_norm(1)
            link(dve.memset(u[:, :, 0:CSTATE], 0.0))
            dve.wait_ge(prep_done, 1)
            link(dve.tensor_copy(v[:, :, NPROMPT:T], vstate[:, :, :]))
            link(dve.tensor_copy(v[:, KD - 1, 0:NPROMPT], chan[:, KD - 1, R_BDW:R_BDW + 1].broadcast_to([P, NPROMPT])))

            def glu(e):
                dve.wait_ge(sig_ready, e + 1)
                dve.scalar_tensor_tensor(out=u[:, e, CSTATE:UW], in0=ps[:, 2 * (e % 4), 0:T], scalar=chan[:, e, R_BA:R_BA + 1],
                                         in1=sg[:, e % 2, :], op0=ALU.add, op1=ALU.mult).then_inc(u_ready, 1)

            def tap(e, j):
                if j == 0:
                    dve.wait_ge(u_ready, e + 1)
                    ins = dve.tensor_scalar(v[:, e, 0:NPROMPT], u[:, e, 0:NPROMPT], chan[:, e, 0:1],
                                            chan[:, e, R_BDW:R_BDW + 1], ALU.mult, ALU.add)
                else:
                    dve.wait_ge(conv_step, CONV_TAPS.index((e, j - 1)) + 1)
                    n = NPROMPT if j < TAPS - 1 else T
                    ins = dve.scalar_tensor_tensor(out=v[:, e, 0:n], in0=u[:, e, j:j + n], scalar=chan[:, e, j:j + 1],
                                                   in1=v[:, e, 0:n], op0=ALU.mult, op1=ALU.add)
                ins.then_inc(conv_step, 1)

            for e, j in CONV_ORDER:
                if j is None:
                    glu(e)
                else:
                    tap(e, j)
            dve.wait_ge(conv_step, CONV_TAPS.index((SHARED, SHARED_TAPS - 1)) + 1)
            for n, e in enumerate((SHARED, KD - 1)):
                dve.wait_ge(diag_summed, n + 1)
                dve.tensor_tensor(out=v[:, e, :], in0=v[:, e, :], in1=ps[:, 7 - 2 * n, 0:T], op=ALU.add).then_inc(conv_done, 1)
            dve.wait_ge(mean_done, 1)
            for g, (t0, tn) in enumerate(GROUPS):
                for k in range(2):
                    vv = v[:, 4 * k:4 * k + 4, t0:t0 + tn]
                    dve.tensor_tensor(out=vv, in0=vv, in1=ps[:, 6, t0:t0 + tn].unsqueeze(1).broadcast_to([P, 4, tn]),
                                      op=ALU.subtract).then_inc(cent_ready, 1)
            dve.wait_ge(cent_ready, 4)
            for g, (t0, tn) in enumerate(GROUPS):
                dve.wait_ge(crt_out, g + 1)
                link(dve.reciprocal(rstd[:, t0:t0 + tn], rstd[:, t0:t0 + tn]))
                for k in range(2):
                    vv = v[:, 4 * k:4 * k + 4, t0:t0 + tn]
                    dve.tensor_tensor(out=vv, in0=vv, in1=rstd[:, t0:t0 + tn].unsqueeze(1).broadcast_to([P, 4, tn]),
                                      op=ALU.mult).then_inc(vn_ready, 1)
            layer_norm(2)
            route(1)
            experts(1)
            overflow(1)
            layer_norm(3)

        @block.tensor
        def _(pe):
            def turn(m, i):
                t0, tn = TILES[i]
                pe.wait_ge(normed, nth(m, i))
                for k in range(KD):
                    bank, at = turn_bank(m, i) + (k // 4 if i < 2 else 0), (k % 4) * P if i < 2 else k * tn
                    mm = pe.transpose(ps[:, bank, at:at + tn], x[0:tn, i, k * P:(k + 1) * P], ident[0:tn, 0:tn])
                    if k % 4 == 3 and (i < 2 or k == 7):
                        mm.then_inc(turned, 1)

            def have_xT(m, i):
                pe.wait_ge(xT_ready, turns(m, i) + (2 if i < 2 else 1))

            def logits(L, i):
                t0, tn = TILES[i]
                if i == 0:
                    pe.wait_ge(wr_in, 32 * (L + 1))
                for k in range(KD):
                    if k % 4 == 0:
                        pe.wait_ge(xT_ready, turns(2 * L, i) + (1 + k // 4 if i < 2 else 1))
                    mm = pe.matmul(ps[0:tn, 6, 36 * i:36 * i + 36], xT[:, k, t0:t0 + tn], wr[:, L, k, :],
                                   start=(k == 0), stop=(k == KD - 1))
                if i == ORDER[2 * L][2]:
                    mm.then_inc(logits_done, 1)

            def stay_warm(count):
                for _ in range(count):
                    pe.matmul(ps[:, 4, 0:P], ident, ones, start=True, stop=True)

            def place(L):
                if L:
                    stay_warm(WARM_BEFORE)
                pe.wait_ge(routed, L + 1)
                for i, (t0, tn) in enumerate(TILES):
                    o = ps[0:tn, 5, NE * i:NE * i + NE]
                    for j in range(i):
                        pe.matmul(o, ones[:, 0:tn], assign[:, j, :], start=(j == 0), stop=False)
                    pe.matmul(o, upper[0:tn, 0:tn], assign[0:tn, i, :], start=(i == 0), stop=True)
                for i, (t0, tn) in enumerate(TILES):
                    mm = pe.matmul(ps[0:1, 5, 3 * NE:4 * NE], ones[0:tn, 0:1], assign[0:tn, i, :],
                                   start=(i == 0), stop=(i == 2))
                mm.then_inc(placed, 1)
                stay_warm(WARM_AFTER)

            def spread_gb(L, k):
                pe.wait_ge(gb_in, 32 * (2 * L + 2))
                pe.matmul(ps[:, 2 + k, :], ones[0:1, :], gb[0:1, k // 2, HALF * (k % 2):HALF * (k % 2) + HALF],
                          start=True, stop=True).then_inc(gb_spread, 1)

            def experts(L):
                def quad(it, b):
                    q = NQ * L + b + 1
                    done = it * TURN + q
                    pe.wait_ge(onehot_ready, done)
                    def dispatch(half):
                        for k in range(4 * half, 4 * half + 4):
                            for i, (t0, tn) in enumerate(TILES):
                                mm = pe.matmul(ps[:, 6 + half, (k % 4) * P:(k % 4 + 1) * P], x[0:tn, i, k * P:(k + 1) * P],
                                               onehot[0:tn, i, :], start=(i == 0), stop=(i == 2))
                        mm.then_inc(dispatched, 1)

                    dispatch(0)
                    pe.wait_ge(xg_a, done)

                    def chunk(c):
                        n = BASE[L] + QCHUNKS * b + c
                        pe.wait_ge(filled[ring_slot(n)], it * TURN_FILLS + fills(n))
                        return ring[:, ring_slot(n), :]

                    for c in range(8):
                        if c == 2:
                            dispatch(1)
                            pe.wait_ge(xg_d, done)
                        w = chunk(c).rearrange("p (e k f) -> p e k f", e=QUAD, k=2)
                        for kk in range(2):
                            k = 2 * (c % 4) + kk
                            for e in range(QUAD):
                                mm = pe.matmul(ps[32 * e:32 * e + 32, c // 4, :], xg[:, k, 32 * e:32 * e + 32],
                                               w[:, e, kk, :], start=(k == 0), stop=(k == KD - 1))
                        mm.then_inc(ring_free, 1)
                        if b == NQ - 1 and c < 4:
                            spread_gb(L, c)
                    if b == NQ - 1:
                        pe.wait_ge(gb_copied, 4 * (L + 1))
                    pe.wait_ge(gated_ready, done)
                    for i, (t0, tn) in enumerate(TILES):
                        mm = pe.transpose(ps[:, 4, t0:t0 + tn], gated[0:tn, i, :], ident[0:tn, 0:tn])
                    mm.then_inc(gT_turned, 1)
                    pe.wait_ge(h_ready, done)
                    for k in range(KF):
                        mm = pe.transpose(ps[:, 5, k * P:(k + 1) * P], h[:, k * P:(k + 1) * P], ident)
                    mm.then_inc(hT_turned, 1)
                    pe.wait_ge(hT_ready, done)
                    for c in range(8, QCHUNKS):
                        w = chunk(c).rearrange("p (e k f) -> p e k f", e=QUAD, k=2)
                        half = (c - 8) // 2
                        for kk in range(2):
                            k = 2 * (c % 2) + kk
                            for e in range(QUAD):
                                mm = pe.matmul(ps[32 * e:32 * e + 32, 2 + half, :], hT[:, k, 32 * e:32 * e + 32],
                                               w[:, e, kk, :], start=(k == 0), stop=(k == KF - 1))
                        mm.then_inc(ring_free, 1)
                        if c % 2 == 0:
                            continue
                        if half == 0:
                            pe.wait_ge(gT_ready, done)
                            pe.wait_ge(ye_a, done)
                        else:
                            pe.wait_ge(ye_d, done)
                        for i, half, bank, at in COMBINE[3 * half:3 * half + 3]:
                            t0, tn = TILES[i]
                            pe.matmul(ps[at:at + tn, bank, :], gT[:, t0:t0 + tn], ye[:, HALF * half:HALF * half + HALF],
                                      start=True, stop=True).then_inc(combined, 1)

                with pe.Fori(0, LOOPS) as it:
                    for b in range(TURN):
                        quad(it, b)
                for b in REST:
                    quad(0, b)

            def overflow(L):
                s = fb[L]
                pe.wait_ge(most_ready, L + 1)
                count = pe.value_load(most[0:1, 0:1], min_val=0, max_val=T)
                with pe.If(count > CAP):
                    pe.wait_ge(added, 6 * NQ * (L + 1))
                    pe.sem_inc(s["used"], 1)
                    for i, (t0, tn) in enumerate(TILES):
                        mm = pe.matmul(ps[0:NE, 5, 0:1], assign[0:tn, i, :], ones[0:tn, 0:1], start=(i == 0), stop=(i == 2))
                    mm.then_inc(s["counts"], 1)
                    pe.wait_ge(s["listed"], 1)
                    pe.matmul(ps[0:NE, 5, 1:2], upper[0:NE, 0:NE], full[:, 0:1], start=True, stop=True).then_inc(s["counts"], 1)
                    pe.wait_ge(s["listed"], 3)
                    pe.matmul(ps[0:1, 5, 2:2 + NE], cst[0:NE, C_NTH:C_NTH + 1], full_at[:, :], start=True, stop=True).then_inc(s["counts"], 1)
                    pe.wait_ge(s["listed"], 5)
                    with pe.Fori(0, NE) as r:
                        with pe.If(listed(pe, r) > 0):
                            for i, (t0, tn) in enumerate(TILES):
                                for m in range(2):
                                    if i == 0:
                                        pe.wait_ge(s[f"fill{m}"], r * 16 + 16)
                                    w = ring[:, m, :].rearrange("p (k f) -> p k f", k=KD)
                                    for k in range(KD):
                                        mm = pe.matmul(ps[0:tn, m, :], xT[:, k, t0:t0 + tn], w[:, k, :], start=(k == 0), stop=(k == KD - 1))
                                mm.then_inc(s["hidden"], 1)
                                pe.wait_ge(s["h"], r * 3 + (i + 1))
                                for k in range(KF):
                                    mm = pe.transpose(ps[:, 5, k * P:(k + 1) * P], h[:, k * P:(k + 1) * P], ident)
                                mm.then_inc(s["turned"], 1)
                                pe.wait_ge(s["hT"], r * 3 + (i + 1))
                                if i == 0:
                                    pe.wait_ge(s["fill2"], r * 16 + 16)
                                w = ring[:, 2, :].rearrange("p (k f) -> p k f", k=KF)
                                for k in range(KF):
                                    for hh in range(2):
                                        mm = pe.matmul(ps[0:tn, 2 + hh, :], hT[:, k, 0:tn], w[:, k, HALF * hh:HALF * hh + HALF],
                                                       start=(k == 0), stop=(k == KF - 1))
                                mm.then_inc(s["down"], 1)
                                pe.wait_ge(s["added"], r * 3 + (i + 1))
                        pe.sem_inc(s["used"], 1)

            pe.wait_ge(x_in, 16 * 7)
            band = lambda at, n, g: bands[:, at + g * n:at + (g + 1) * n]
            for c in range(KD):
                g, cols = c // 2, slice(c * P, (c + 1) * P)
                o = ps[:, c, :]
                pe.matmul(o[:, 0:144], x[:, 0, cols], band(B_0, 144, g), start=True, stop=False, skip_group_check=True)
                pe.matmul(o[:, 128:272], x[:, 1, cols], band(B_1, 144, g), start=False, stop=False, skip_group_check=True)
                pe.matmul(o[:, 272:280], pstate[0:120, cols], band(B_S, 8, g)[0:120, :], start=False, stop=False,
                          skip_group_check=True)
                pe.matmul(o[:, 256:280], x[0:24, 2, cols], band(B_2, 24, g)[0:24, :], start=False, stop=True,
                          skip_group_check=True).then_inc(diff_done, 1)
            pe.wait_ge(diff_a, 4)
            pe.wait_ge(diff_d, 4)
            for i, (t0, tn) in enumerate(TILES):
                for g in range(NPG):
                    for k in range(2):
                        mm = pe.matmul(ps[0:tn, 2 * i + g // 2, (g % 2) * PGD:(g % 2 + 1) * PGD], xT[:, 2 * g + k, t0:t0 + tn],
                                       wp[:, g, k, :], start=(k == 0), stop=(k == 1))
                mm.then_inc(pooled, 1)
            pe.wait_ge(prep_in, 16 * 11)
            for k in range(KD):
                mm = pe.transpose(ps[:, 7, k * R_N:(k + 1) * R_N], crow[:, k * P:(k + 1) * P], ident[0:R_N, 0:R_N])
            mm.then_inc(chan_turned, 1)

            def state_taps(hh):
                pe.wait_ge(state_mul, hh + 1)
                for k in range(KD):
                    at = KD * R_N + k * NSAMP + 4 * hh
                    mm = pe.matmul(ps[:, 7, at:at + 4], cs_raw[0:120, hh, k * P:(k + 1) * P],
                                   cst[0:120, C_SELB:C_SELB + 4], start=True, stop=True)
                mm.then_inc(vstate_done, 1)

            state_taps(0)
            turn(0, 0)
            turn(0, 1)
            logits(0, 0)
            logits(0, 1)
            turn(0, 2)
            logits(0, 2)
            state_taps(1)
            place(0)
            experts(0)
            overflow(0)
            def glu(e, t0, tn, halves=(0, 1)):
                n = MIX_BASE + e // 2
                if e % 2 == 0:
                    pe.wait_ge(filled[ring_slot(n)], fills(n))
                w = ring[:, ring_slot(n), :].rearrange("p (k h n) -> p k h n", k=KD, h=2)
                for hh in halves:
                    for k in range(KD):
                        mm = pe.matmul(ps[:, 2 * (e % 4) + hh, t0:t0 + tn], w[:, k, hh, (e % 2) * P:(e % 2 + 1) * P],
                                       xT[:, k, t0:t0 + tn], start=(k == 0), stop=(k == KD - 1), skip_group_check=True)
                return mm

            turn(1, 0)
            have_xT(1, 0)
            glu(0, 0, P, halves=(0,))
            turn(1, 1)
            glu(0, 0, P, halves=(1,))
            turn(1, 2)
            have_xT(1, 2)
            glu(0, P, T - P).then_inc(glu_done, 1)
            for e in range(1, KD):
                if e >= 4:
                    pe.wait_ge(u_ready, e - 3)
                glu(e, 0, T).then_inc(ring_free if e % 2 else glu_done, 1)

            def mean(k):
                if k < SHARED:
                    pe.wait_ge(conv_step, CONV_TAPS.index((k, TAPS - 1)) + 1)
                else:
                    pe.wait_ge(conv_done, k - SHARED + 1)
                return pe.matmul(ps[:, 6, 0:T], mean_w, v[:, k, :], start=(k == 0), stop=(k == KD - 1))

            def pw_bias(i):
                tn = TILES[i][1]
                for hh in range(2):
                    at, bank = (32 * hh, 4) if i == 2 else (0, 2 * i + hh)
                    pe.matmul(ps[at:at + tn, bank, :], ones[32:33, 0:tn], bpw[:, HALF * hh:HALF * hh + HALF],
                              start=True, stop=False)

            for m, (e, j) in enumerate(DIAG_TAPS):
                first, last = j == (SHARED_TAPS if e == SHARED else 0), j == TAPS - 1
                if first:
                    pe.wait_ge(u_ready, e + 1 if e == KD - 1 else KD - 1)
                pe.wait_ge(diag_ready, m + 1)
                n = NPROMPT if not last else T
                pe.matmul(ps[:, 7 if e == SHARED else 5, 0:n], diag[:, m % NDIAG, :], u[:, e, j:j + n], start=first, stop=last,
                          skip_group_check=True).then_inc(diag_summed if last else diag_used, 1)
                if last and e == SHARED:
                    pe.wait_ge(u_ready, KD)
                    for k in range(KD):
                        mm = pe.matmul(ps[64 * (k // 4):64 * (k // 4) + 38, 4, (k % 4) * P:(k % 4 + 1) * P],
                                       u[:, k, UW - 38:UW], ident, start=True, stop=True)
                        if k % 4 == 3:
                            mm.then_inc(urow_turned, 1)
                    pw_bias(0)
                    pw_bias(1)
                    mean(0)
                    mean(1)

            for k in range(2, KD):
                mm = mean(k)
            mm.then_inc(mean_done, 1)
            pe.wait_ge(urow_ready, 2)
            pw_bias(2)
            for g, (t0, tn) in enumerate(GROUPS):
                for k in range(KD):
                    if k % 4 == 0:
                        pe.wait_ge(sq_ready, 2 * g + k // 4 + 1)
                    mm = pe.matmul(ps[:, 7 - 2 * g, 0:tn], mean_w, sq[:, k, t0:t0 + tn], start=(k == 0), stop=(k == KD - 1))
                mm.then_inc(var_done, 1)

            def pointwise(i):
                t0, tn = TILES[i]
                steps = [(k, hh) for k in range(KD) for hh in range(2)] if i == 2 else [(k, hh) for hh in range(2) for k in range(KD)]
                for k, hh in steps:
                    n = MIX_BASE + 4 + k // 4
                    if i == 0 and hh == 0:
                        pe.wait_ge(act_ready, k + 1)
                        if k % 4 == 0:
                            pe.wait_ge(filled[ring_slot(n)], fills(n))
                    elif i == 2:
                        pe.wait_ge(act_ready, 2 * KD)
                    w = ring[:, ring_slot(n), :].rearrange("p (k n) -> p k n", k=4)
                    at, bank = (64 * (k % 2) + 32 * hh, 4) if i == 2 else (0, 2 * i + hh)
                    mm = pe.matmul(ps[at:at + tn, bank, :], sq[:, k, t0:t0 + tn], w[:, k % 4, HALF * hh:HALF * hh + HALF],
                                   start=(i == 2 and k == 1), stop=(k == KD - 1 or i == 2 and k == KD - 2))
                    if i == 1 and hh == 1 and k % 4 == 3:
                        mm.then_inc(ring_free, 1)
                    elif i < 2 and k == KD - 1 or (k, hh) == steps[-1]:
                        mm.then_inc(pw_done, 1)

            pointwise(0)
            pointwise(2)
            pointwise(1)
            turn(2, 0)
            turn(2, 2)
            logits(1, 0)
            logits(1, 2)
            turn(2, 1)
            logits(1, 1)
            place(1)
            experts(1)
            overflow(1)


_INS = ["x_prompt", "x_sample", "state_pool", "state_conv", "meta", "w_pool", "pool_scale", "w_glu", "b_glu", "w_dw",
        "b_dw", "conv_ln_g", "conv_ln_b", "w_pw", "b_pw", "ln_mix_g", "ln_mix_b", "ln_ffn_g", "ln_ffn_b",
        "w_router_group", "w_router_expert", "w_gate", "w_up", "w_down"]
_OUTS = [(1, SEQ, D), (NSAMP, 1, D), (1, 1, PSTATE, D), (1, NSAMP, PSTATE, D), (1, 1, CSTATE, D), (1, NSAMP, CSTATE, D)]


def kernel(**inputs):
    import concourse.bacc as _bacc
    from concourse.bass_utils import run_bass_kernel_spmd as _run

    nc = _bacc.Bacc("TRN2", target_bir_lowering=False, num_devices=1)
    arrays, args = {}, {}
    cst, bands = constants()
    for name, arr in [(n, inputs[n]) for n in _INS] + [("cst", cst), ("bands", bands)]:
        arr = np.ascontiguousarray(arr)
        arrays[f"in_{name}"] = arr
        args[name] = nc.dram_tensor(f"in_{name}", arr.shape, mybir.dt.from_np(arr.dtype), kind="ExternalInput").ap()
    outs = [nc.dram_tensor(f"out_{i}", s, mybir.dt.float32, kind="ExternalOutput").ap() for i, s in enumerate(_OUTS)]
    build(nc, args, outs)
    r = _run(nc, [arrays], core_ids=[0])
    return tuple(r.results[0][f"out_{i}"] for i in range(len(_OUTS)))
```
